# Optimizing a Trainium2 kernel written in Bass

```python
import jax, jax.numpy as jnp
from jax import lax
import numpy as np
import math
import jax
import jax.numpy as jnp

D_MODEL = 1024
BATCH = 1
SEQ = 512
DEPTH = 1

CHUNK = 64
N_MEM = 256
GDN_HEAD_DIM = 128
GDN_WIDTH = D_MODEL
GDN_HEADS = GDN_WIDTH // GDN_HEAD_DIM
CONV_WIDTH = 4
GLA_HEADS = 4
GLA_KEY_WIDTH = D_MODEL // 2
GLA_VAL_WIDTH = D_MODEL
GLA_KEY_DIM = GLA_KEY_WIDTH // GLA_HEADS
GLA_VAL_DIM = GLA_VAL_WIDTH // GLA_HEADS
GLA_GATE_RANK = 16
GLA_GATE_TAU = 16.0
XATTN_HEADS = 4
XATTN_HEAD_DIM = D_MODEL // XATTN_HEADS
D_FF = 4 * D_MODEL
NORM_EPS = 1e-6
IN_SIZES = (GDN_WIDTH, GDN_WIDTH, GDN_WIDTH, GDN_WIDTH, GDN_HEADS, GDN_HEADS,
            GLA_KEY_WIDTH, GLA_KEY_WIDTH, GLA_VAL_WIDTH, GLA_VAL_WIDTH, GLA_GATE_RANK,
            D_MODEL, D_MODEL)
IN_WIDTH = 4 * GDN_WIDTH + 2 * GDN_HEADS + 2 * GLA_KEY_WIDTH + 2 * GLA_VAL_WIDTH + GLA_GATE_RANK + 2 * D_MODEL


def rmsnorm(x, g):
    xf = x.astype(jnp.float32)
    y = xf * lax.rsqrt(jnp.mean(xf * xf, axis=-1, keepdims=True) + NORM_EPS)
    return (y * g.astype(jnp.float32)).astype(x.dtype)

def l2norm(x):
    return x * lax.rsqrt(jnp.sum(x * x, axis=-1, keepdims=True) + NORM_EPS)

def causal_depthwise_conv(x, w):
    c = x.shape[-1]
    return lax.conv_general_dilated(
        x, w.astype(x.dtype)[:, None, :], window_strides=(1,),
        padding=[(w.shape[0] - 1, 0)], dimension_numbers=("NWC", "WIO", "NWC"),
        feature_group_count=c)

def to_chunks(t, n_heads):
    b, s, _ = t.shape
    return t.reshape(b, s // CHUNK, CHUNK, n_heads, -1).transpose(0, 3, 1, 2, 4)

def scalar_chunks(t):
    b, s, h = t.shape
    return t.reshape(b, s // CHUNK, CHUNK, h).transpose(0, 3, 1, 2)

def from_chunks(t):
    b, h, n, c, d = t.shape
    return t.transpose(0, 2, 3, 1, 4).reshape(b, n * c, h, d)

def gated_delta_rule_chunked(q, k, v, g, beta):
    dk, dv = k.shape[-1], v.shape[-1]
    idx = jnp.arange(CHUNK)
    strict = idx[:, None] > idx[None, :]
    incl = idx[:, None] >= idx[None, :]
    gc = jnp.cumsum(g, axis=-1)
    decay = jnp.exp(jnp.where(incl, gc[..., :, None] - gc[..., None, :], -jnp.inf))
    kk = jnp.einsum('bhnid,bhnjd->bhnij', k, k)
    lower = jnp.where(strict, beta[..., :, None] * kk * decay, 0.0)
    rhs = jnp.concatenate([beta[..., None] * v, (beta * jnp.exp(gc))[..., None] * k], axis=-1)
    sol = lax.linalg.triangular_solve(lower, rhs, left_side=True, lower=True, unit_diagonal=True)
    u, w = sol[..., :dv], sol[..., dv:]
    a_qk = jnp.einsum('bhnid,bhnjd->bhnij', q, k) * decay
    q_dec = q * jnp.exp(gc)[..., None]
    k_dec = k * jnp.exp(gc[..., -1:] - gc)[..., None]
    g_end = jnp.exp(gc[..., -1])
    xs = tuple(jnp.moveaxis(t, 2, 0) for t in (u, w, q_dec, a_qk, k_dec, g_end))

    def step(state, inp):
        u_c, w_c, q_c, a_c, k_c, ge = inp
        delta = u_c - jnp.einsum('bhcd,bhde->bhce', w_c, state)
        o = jnp.einsum('bhcd,bhde->bhce', q_c, state) + jnp.einsum('bhij,bhje->bhie', a_c, delta)
        state = ge[..., None, None] * state + jnp.einsum('bhcd,bhce->bhde', k_c, delta)
        return state, o

    s0 = jnp.zeros(q.shape[:2] + (dk, dv), q.dtype)
    _, o = lax.scan(step, s0, xs)
    return jnp.moveaxis(o, 0, 2)

def gla_chunked(q, k, v, gk):
    dk, dv = k.shape[-1], v.shape[-1]
    idx = jnp.arange(CHUNK)
    incl = idx[:, None] >= idx[None, :]
    bc = jnp.cumsum(gk, axis=-2)
    b_ref = bc[..., CHUNK // 2:CHUNK // 2 + 1, :]
    a_qk = jnp.einsum('bhnid,bhnjd->bhnij', q * jnp.exp(bc - b_ref), k * jnp.exp(b_ref - bc))
    o_intra = jnp.einsum('bhnij,bhnje->bhnie', jnp.where(incl, a_qk, 0.0), v)
    q_dec = q * jnp.exp(bc)
    k_dec = k * jnp.exp(bc[..., -1:, :] - bc)
    g_end = jnp.exp(bc[..., -1, :])
    xs = tuple(jnp.moveaxis(t, 2, 0) for t in (q_dec, o_intra, k_dec, v, g_end))

    def step(state, inp):
        q_c, oi_c, k_c, v_c, ge = inp
        o = jnp.einsum('bhcd,bhde->bhce', q_c, state) + oi_c
        state = ge[..., :, None] * state + jnp.einsum('bhcd,bhce->bhde', k_c, v_c)
        return state, o

    s0 = jnp.zeros(q.shape[:2] + (dk, dv), q.dtype)
    _, o = lax.scan(step, s0, xs)
    return jnp.moveaxis(o, 0, 2)

def first_inputs(seed: int = 0) -> dict:
    key = jax.random.key(seed)
    ks = iter(jax.random.split(key, 32))
    nrm = lambda shape, scale: jax.random.normal(next(ks), shape, jnp.float32) * scale
    gain = lambda n: 1.0 + nrm((DEPTH, n), 0.02)
    a_log = jnp.log(jax.random.uniform(next(ks), (DEPTH, GDN_HEADS), jnp.float32, 1.0, 16.0))
    dt = jnp.exp(jax.random.uniform(next(ks), (DEPTH, GDN_HEADS), jnp.float32, np.log(1e-3), np.log(1e-1)))
    dt_bias = dt + jnp.log(-jnp.expm1(-dt))
    return {
        "x": nrm((BATCH, SEQ, D_MODEL), 1.0),
        "mem": nrm((BATCH, N_MEM, D_MODEL), 1.0),
        "norm_mix_g": gain(D_MODEL),
        "w_in": nrm((DEPTH, D_MODEL, IN_WIDTH), D_MODEL ** -0.5),
        "gdn_conv_w": nrm((DEPTH, CONV_WIDTH, 3 * GDN_WIDTH), CONV_WIDTH ** -0.5),
        "gdn_a_log": a_log,
        "gdn_dt_bias": dt_bias,
        "gdn_norm_g": gain(GDN_HEAD_DIM),
        "gla_w_gate2": nrm((DEPTH, GLA_GATE_RANK, GLA_KEY_WIDTH), GLA_GATE_RANK ** -0.5),
        "gla_b_gate": nrm((DEPTH, GLA_KEY_WIDTH), 0.1),
        "gla_norm_g": gain(GLA_VAL_DIM),
        "w_branch_gdn": nrm((DEPTH, GDN_WIDTH, D_MODEL), GDN_WIDTH ** -0.5),
        "w_branch_gla": nrm((DEPTH, GLA_VAL_WIDTH, D_MODEL), GLA_VAL_WIDTH ** -0.5),
        "w_out": nrm((DEPTH, D_MODEL, D_MODEL), D_MODEL ** -0.5),
        "norm_xattn_g": gain(D_MODEL),
        "norm_mem_g": gain(D_MODEL),
        "xattn_wq": nrm((DEPTH, D_MODEL, D_MODEL), D_MODEL ** -0.5),
        "xattn_wk": nrm((DEPTH, D_MODEL, D_MODEL), D_MODEL ** -0.5),
        "xattn_wv": nrm((DEPTH, D_MODEL, D_MODEL), D_MODEL ** -0.5),
        "xattn_wo": nrm((DEPTH, D_MODEL, D_MODEL), D_MODEL ** -0.5),
        "norm_mlp_g": gain(D_MODEL),
        "mlp_w1": nrm((DEPTH, D_MODEL, D_FF), D_MODEL ** -0.5),
        "mlp_w2": nrm((DEPTH, D_FF, D_MODEL), D_FF ** -0.5),
        "norm_final_g": 1.0 + nrm((D_MODEL,), 0.02),
    }

def first_block(x, mem, norm_mix_g, w_in, gdn_conv_w, gdn_a_log, gdn_dt_bias, gdn_norm_g,
              gla_w_gate2, gla_b_gate, gla_norm_g, w_branch_gdn, w_branch_gla, w_out,
              norm_xattn_g, norm_mem_g, xattn_wq, xattn_wk, xattn_wv, xattn_wo,
              norm_mlp_g, mlp_w1, mlp_w2, norm_final_g):
    dt = x.dtype
    f32 = jnp.float32
    bsz, seq, _ = x.shape
    split_at = [int(v) for v in np.cumsum(IN_SIZES)[:-1]]
    for i in range(DEPTH):
        h = rmsnorm(x, norm_mix_g[i])
        proj = h @ w_in[i].astype(dt)
        (gq, gk_, gv, gz, ga, gb, lq, lk, lv, lr, lgate, gate_a, gate_b) = jnp.split(proj, split_at, axis=-1)

        qkv = jax.nn.silu(causal_depthwise_conv(jnp.concatenate([gq, gk_, gv], -1), gdn_conv_w[i]))
        cq, ck, cv = jnp.split(qkv.astype(f32), [GDN_WIDTH, 2 * GDN_WIDTH], axis=-1)
        q_a = l2norm(to_chunks(cq, GDN_HEADS)) * (GDN_HEAD_DIM ** -0.5)
        k_a = l2norm(to_chunks(ck, GDN_HEADS))
        v_a = to_chunks(cv, GDN_HEADS)
        g_a = -jnp.exp(gdn_a_log[i].astype(f32)) * jax.nn.softplus(ga.astype(f32) + gdn_dt_bias[i].astype(f32))
        beta_a = jax.nn.sigmoid(gb.astype(f32))
        o_a = gated_delta_rule_chunked(q_a, k_a, v_a, scalar_chunks(g_a), scalar_chunks(beta_a))
        o_a = rmsnorm(from_chunks(o_a).astype(dt), gdn_norm_g[i]) * jax.nn.silu(gz.reshape(bsz, seq, GDN_HEADS, GDN_HEAD_DIM))
        y_a = o_a.reshape(bsz, seq, GDN_WIDTH) @ w_branch_gdn[i].astype(dt)

        log_fg = jax.nn.log_sigmoid((lgate @ gla_w_gate2[i].astype(dt)).astype(f32) + gla_b_gate[i].astype(f32)) / GLA_GATE_TAU
        q_b = to_chunks(lq.astype(f32), GLA_HEADS) * (GLA_KEY_DIM ** -0.5)
        k_b = to_chunks(lk.astype(f32), GLA_HEADS)
        v_b = to_chunks(lv.astype(f32), GLA_HEADS)
        o_b = gla_chunked(q_b, k_b, v_b, to_chunks(log_fg, GLA_HEADS))
        o_b = rmsnorm(from_chunks(o_b).astype(dt), gla_norm_g[i]) * jax.nn.silu(lr.reshape(bsz, seq, GLA_HEADS, GLA_VAL_DIM))
        y_b = o_b.reshape(bsz, seq, GLA_VAL_WIDTH) @ w_branch_gla[i].astype(dt)

        merged = jax.nn.sigmoid(gate_a) * y_a + jax.nn.sigmoid(gate_b) * y_b
        x = x + merged @ w_out[i].astype(dt)

        h = rmsnorm(x, norm_xattn_g[i])
        m = rmsnorm(mem.astype(dt), norm_mem_g[i])
        q = (h @ xattn_wq[i].astype(dt)).reshape(bsz, seq, XATTN_HEADS, XATTN_HEAD_DIM)
        k = (m @ xattn_wk[i].astype(dt)).reshape(bsz, -1, XATTN_HEADS, XATTN_HEAD_DIM)
        v = (m @ xattn_wv[i].astype(dt)).reshape(bsz, -1, XATTN_HEADS, XATTN_HEAD_DIM)
        s = jnp.einsum('bshd,bmhd->bhsm', q, k).astype(f32) * (XATTN_HEAD_DIM ** -0.5)
        p = jax.nn.softmax(s, axis=-1).astype(dt)
        o = jnp.einsum('bhsm,bmhd->bshd', p, v).reshape(bsz, seq, D_MODEL)
        x = x + o @ xattn_wo[i].astype(dt)

        h = rmsnorm(x, norm_mlp_g[i])
        x = x + jnp.square(jax.nn.relu(h @ mlp_w1[i].astype(dt))) @ mlp_w2[i].astype(dt)
    return rmsnorm(x, norm_final_g)


DEPTH_2 = 2

GRID_W = 64
CTX_LEN = 256
N_MIXERS = 4
HEAD_DIM = 64
ROPE_BASE = 10000.0
RMS_EPS = 1e-6
D_FF_2 = ((8 * D_MODEL // 3 + 255) // 256) * 256
N_MOD = 6

DA_HEADS = D_MODEL // (2 * HEAD_DIM)
DA_VDIM = 2 * HEAD_DIM
Q_BLOCK = 128

SC_WIDTH = 3

WA_HEADS = D_MODEL // HEAD_DIM
WA_KV_HEADS = 4
WINDOW = 128
W_BLOCK = WINDOW

HG_EXPAND = 128
HG_HEADS = D_MODEL // HG_EXPAND
HG_DK = HG_EXPAND
HG_DV = D_MODEL // HG_HEADS
HG_FDIM = HG_HEADS * HG_DK


def n_layers_of(mixer):
    return len(range(mixer, DEPTH_2, N_MIXERS))

def rmsnorm_2(x, g):
    x32 = x.astype(jnp.float32)
    y = x32 * lax.rsqrt(jnp.mean(x32 * x32, axis=-1, keepdims=True) + RMS_EPS)
    return y.astype(x.dtype) * g

def modulate(x, shift, scale):
    return x * (1.0 + scale) + shift

def swiglu(t, w_in, w_out):
    a, b = jnp.split(t @ w_in, 2, axis=-1)
    return (jax.nn.silu(a) * b) @ w_out

def rope_tables(n_tokens):
    rows = n_tokens // GRID_W
    row = jnp.repeat(jnp.arange(rows), GRID_W).astype(jnp.float32)
    col = jnp.tile(jnp.arange(GRID_W), rows).astype(jnp.float32)
    half = HEAD_DIM // 2
    inv_freq = 1.0 / (ROPE_BASE ** (jnp.arange(0, half, 2, dtype=jnp.float32) / half))
    ang = jnp.concatenate([row[:, None] * inv_freq, col[:, None] * inv_freq], axis=-1)
    return jnp.cos(ang), jnp.sin(ang)

def apply_rope_2d(x, cos, sin):
    n_mid = x.ndim - 3
    qd = HEAD_DIM // 4
    bshape = (cos.shape[0],) + (1,) * n_mid + (2, qd)
    cs, sn = cos.reshape(bshape), sin.reshape(bshape)
    xs = x.reshape(x.shape[:-1] + (2, 2, qd))
    x1, x2 = xs[..., 0, :], xs[..., 1, :]
    out = jnp.stack([x1 * cs - x2 * sn, x2 * cs + x1 * sn], axis=-2)
    return out.reshape(x.shape)

def sink_softmax(scores, sink):
    m = sink
    for s in scores:
        m = jnp.maximum(m, jnp.max(s, axis=-1, keepdims=True))
    es = [jnp.exp(s - m) for s in scores]
    den = jnp.exp(sink - m)
    for e in es:
        den = den + jnp.sum(e, axis=-1, keepdims=True)
    return [e / den for e in es]

def diff_attention(h, hc, wqkv, lam, subln_g, wo, cos, sin, layer_idx, need_ctx):
    B, L, _ = h.shape
    lam_init = 0.8 - 0.6 * math.exp(-0.3 * layer_idx)
    lam32 = lam.astype(jnp.float32)
    lam_full = (jnp.exp(jnp.sum(lam32[0] * lam32[1]))
                - jnp.exp(jnp.sum(lam32[2] * lam32[3])) + lam_init)
    scale = HEAD_DIM ** -0.5

    def project(t):
        n = t.shape[1]
        q, k, v = jnp.split(t @ wqkv, 3, axis=-1)
        return (q.reshape(B, n, DA_HEADS, 2, HEAD_DIM),
                k.reshape(B, n, DA_HEADS, 2, HEAD_DIM),
                v.reshape(B, n, DA_HEADS, DA_VDIM))

    def attend(qb, kk, vv):
        s = jnp.einsum('bqhmd,bkhmd->bhmqk', qb, kk).astype(jnp.float32) * scale
        p = jax.nn.softmax(s, axis=-1)
        p = p[:, :, 0] - lam_full * p[:, :, 1]
        return jnp.einsum('bhqk,bkhe->bqhe', p.astype(vv.dtype), vv)

    def readout(o):
        n = o.shape[1]
        o = rmsnorm_2(o, subln_g) * (1.0 - lam_init)
        return o.reshape(B, n, D_MODEL) @ wo

    q, k, v = project(h)
    q, k = apply_rope_2d(q, cos, sin), apply_rope_2d(k, cos, sin)
    qc, kc, vc = project(hc)
    k_all = jnp.concatenate([kc, k], axis=1)
    v_all = jnp.concatenate([vc, v], axis=1)
    nb = L // Q_BLOCK
    q_blocks = jnp.moveaxis(q.reshape(B, nb, Q_BLOCK, DA_HEADS, 2, HEAD_DIM), 1, 0)
    o = lax.map(lambda qb: attend(qb, k_all, v_all), q_blocks)
    o = jnp.moveaxis(o, 0, 1).reshape(B, L, DA_HEADS, DA_VDIM)
    y = readout(o)
    yc = readout(attend(qc, kc, vc)) if need_ctx else None
    return yc, y

def short_conv(h, hc, w_in, conv_w, w_out, need_ctx):
    pad = SC_WIDTH // 2

    def run(t):
        n = t.shape[1]
        b_gate, c_gate, u = jnp.split(t @ w_in, 3, axis=-1)
        z = c_gate * u
        zp = jnp.pad(z, ((0, 0), (pad, pad), (0, 0)))
        conv = conv_w[0] * zp[:, 0:n]
        for j in range(1, SC_WIDTH):
            conv = conv + conv_w[j] * zp[:, j:j + n]
        return (b_gate * conv) @ w_out

    y = run(h)
    yc = run(hc) if need_ctx else None
    return yc, y

def window_attention(h, hc, wqkv, sinks, wo, cos, sin, need_ctx):
    B, L, _ = h.shape
    G, R = WA_KV_HEADS, WA_HEADS // WA_KV_HEADS
    scale = HEAD_DIM ** -0.5
    qw, kw = WA_HEADS * HEAD_DIM, WA_KV_HEADS * HEAD_DIM

    def project(t):
        n = t.shape[1]
        qkv = t @ wqkv
        q = qkv[..., :qw].reshape(B, n, G, R, HEAD_DIM)
        k = qkv[..., qw:qw + kw].reshape(B, n, G, HEAD_DIM)
        v = qkv[..., qw + kw:].reshape(B, n, G, HEAD_DIM)
        return q, k, v

    sink = sinks.reshape(G, R).astype(jnp.float32)
    q, k, v = project(h)
    q, k = apply_rope_2d(q, cos, sin), apply_rope_2d(k, cos, sin)
    qc, kc, vc = project(hc)

    nb = L // W_BLOCK
    qb = q.reshape(B, nb, W_BLOCK, G, R, HEAD_DIM)

    def band(a):
        ab = jnp.pad(a.reshape(B, nb, W_BLOCK, G, HEAD_DIM), ((0, 0), (1, 1), (0, 0), (0, 0), (0, 0)))
        return jnp.concatenate([ab[:, :-2], ab[:, 1:-1], ab[:, 2:]], axis=2)

    kb, vb = band(k), band(v)
    q_pos = jnp.arange(nb)[:, None] * W_BLOCK + jnp.arange(W_BLOCK)[None, :]
    k_pos = (jnp.arange(nb)[:, None] - 1) * W_BLOCK + jnp.arange(3 * W_BLOCK)[None, :]
    rel = k_pos[:, None, :] - q_pos[:, :, None]
    valid = (jnp.abs(rel) <= WINDOW) & (k_pos[:, None, :] >= 0) & (k_pos[:, None, :] < L)

    s_win = jnp.einsum('bnqgrd,bnkgd->bngrqk', qb, kb).astype(jnp.float32) * scale
    s_win = jnp.where(valid[None, :, None, None], s_win, -jnp.inf)
    s_ctx = jnp.einsum('bnqgrd,bcgd->bngrqc', qb, kc).astype(jnp.float32) * scale
    p_ctx, p_win = sink_softmax([s_ctx, s_win], sink[None, None, :, :, None, None])
    o = (jnp.einsum('bngrqc,bcgd->bnqgrd', p_ctx.astype(vc.dtype), vc)
         + jnp.einsum('bngrqk,bnkgd->bnqgrd', p_win.astype(vb.dtype), vb))
    y = o.reshape(B, L, D_MODEL) @ wo

    yc = None
    if need_ctx:
        n = hc.shape[1]
        s_c = jnp.einsum('bqgrd,bcgd->bgrqc', qc, kc).astype(jnp.float32) * scale
        (p_c,) = sink_softmax([s_c], sink[None, :, :, None, None])
        oc = jnp.einsum('bgrqc,bcgd->bqgrd', p_c.astype(vc.dtype), vc)
        yc = oc.reshape(B, n, D_MODEL) @ wo
    return yc, y

def gla_scan(q, k, v, logf, s0, with_output):
    B, NH, T, _ = q.shape
    nc = T // CHUNK

    def chunks(a):
        return jnp.moveaxis(a.astype(jnp.float32).reshape(B, NH, nc, CHUNK, a.shape[-1]), 2, 0)

    tri = jnp.tril(jnp.ones((CHUNK, CHUNK), dtype=bool))[:, :, None]

    def step(S, xs):
        qc, kc, vc, gc = xs
        b = jnp.cumsum(gc, axis=2)
        b_end = b[:, :, -1:, :]
        S_next = (jnp.exp(b_end)[:, :, 0, :, None] * S
                  + jnp.einsum('bhsk,bhsv->bhkv', kc * jnp.exp(b_end - b), vc))
        if not with_output:
            return S_next, None
        rel = jnp.where(tri, b[:, :, :, None, :] - b[:, :, None, :, :], -jnp.inf)
        att = jnp.sum(qc[:, :, :, None, :] * kc[:, :, None, :, :] * jnp.exp(rel), axis=-1)
        o = att @ vc + jnp.einsum('bhtk,bhkv->bhtv', qc * jnp.exp(b), S)
        return S_next, o

    S_fin, o = lax.scan(step, s0, (chunks(q), chunks(k), chunks(v), chunks(logf)))
    if not with_output:
        return S_fin, None
    return S_fin, jnp.moveaxis(o, 0, 2).reshape(B, NH, T, v.shape[-1])

def hgrn2(h, hc, w_in, lb_param, gnorm_g, wo, layer_idx, need_ctx):
    B = h.shape[0]
    H = HG_HEADS
    p = jax.nn.softmax(lb_param.astype(jnp.float32), axis=1)
    lb = (jnp.cumsum(p, axis=1) - p[:, :1])[:, layer_idx][:, None, None, :]

    def gates(t):
        q, f_fw, f_bw, i_in, og = jnp.split(t @ w_in, 5, axis=-1)
        q = jax.nn.silu(q)
        f_pre = jnp.stack([f_fw, f_bw], axis=0).astype(jnp.float32)
        logf = jnp.logaddexp(jnp.log(lb), jnp.log1p(-lb) + jax.nn.log_sigmoid(f_pre))
        k = -jnp.expm1(logf)
        return q, k, i_in, logf, og

    def to_heads(a):
        return a.reshape(a.shape[0], a.shape[1], H, -1).transpose(0, 2, 1, 3)

    def both(a_fw, a_bw):
        return jnp.concatenate([to_heads(a_fw), jnp.flip(to_heads(a_bw), axis=2)], axis=1)

    def merge(o):
        return (o[:, :H] + jnp.flip(o[:, H:], axis=2)).transpose(0, 2, 1, 3)

    def readout(o, og):
        n = o.shape[1]
        o = rmsnorm_2(o.astype(h.dtype), gnorm_g) * jax.nn.silu(og).reshape(B, n, H, HG_DV)
        return o.reshape(B, n, D_MODEL) @ wo

    qc, kc, vc, gc, ogc = gates(hc)
    s0 = jnp.zeros((B, 2 * H, HG_DK, HG_DV), jnp.float32)
    S_ctx, o_ctx = gla_scan(both(qc, qc), both(kc[0], kc[1]), both(vc, vc), both(gc[0], gc[1]),
                            s0, need_ctx)
    q, k, v, g, og = gates(h)
    _, o = gla_scan(both(q, q), both(k[0], k[1]), both(v, v), both(g[0], g[1]), S_ctx, True)
    y = readout(merge(o), og)
    yc = readout(merge(o_ctx), ogc) if need_ctx else None
    return yc, y

def second_inputs(seed: int = 0) -> dict:
    key = jax.random.key(seed)
    keys = jax.random.split(key, 32)
    counter = [0]

    def nrm(shape, scale):
        k = keys[counter[0]]
        counter[0] += 1
        return jax.random.normal(k, shape, jnp.float32) * scale

    D, F = D_MODEL, D_FF_2
    nA, nB, nC, nD = n_layers_of(0), n_layers_of(1), n_layers_of(2), n_layers_of(3)
    wa_cols = (WA_HEADS + 2 * WA_KV_HEADS) * HEAD_DIM
    return {
        'x': nrm((BATCH, SEQ, D), 1.0),
        'c': nrm((BATCH, D), 1.0),
        'ctx': nrm((BATCH, CTX_LEN, D), 1.0),
        'c_ctx': nrm((D,), 1.0),
        'ada_w': nrm((DEPTH_2, D, N_MOD * D), 0.5 * D ** -0.5),
        'ada_b': nrm((DEPTH_2, N_MOD * D), 0.02),
        'norm1_g': 1.0 + nrm((DEPTH_2, D), 0.02),
        'norm2_g': 1.0 + nrm((DEPTH_2, D), 0.02),
        'ffn_w_in': nrm((DEPTH_2, D, 2 * F), D ** -0.5),
        'ffn_w_out': nrm((DEPTH_2, F, D), F ** -0.5),
        'final_g': 1.0 + nrm((D,), 0.02),
        'da_wqkv': nrm((nA, D, 3 * D), D ** -0.5),
        'da_lambda': nrm((nA, 4, HEAD_DIM), 0.1),
        'da_subln_g': 1.0 + nrm((nA, DA_VDIM), 0.02),
        'da_wo': nrm((nA, D, D), D ** -0.5),
        'sc_w_in': nrm((nB, D, 3 * D), D ** -0.5),
        'sc_conv_w': nrm((nB, SC_WIDTH, D), SC_WIDTH ** -0.5),
        'sc_w_out': nrm((nB, D, D), D ** -0.5),
        'wa_wqkv': nrm((nC, D, wa_cols), D ** -0.5),
        'wa_sinks': nrm((nC, WA_HEADS), 0.5),
        'wa_wo': nrm((nC, WA_HEADS * HEAD_DIM, D), D ** -0.5),
        'hg_w_in': nrm((nD, D, 5 * D), D ** -0.5),
        'hg_lb': nrm((2, DEPTH_2, HG_FDIM), 0.1),
        'hg_gnorm_g': 1.0 + nrm((nD, HG_DV), 0.02),
        'hg_wo': nrm((nD, D, D), D ** -0.5),
    }

def second_block(x, c, ctx, c_ctx, ada_w, ada_b, norm1_g, norm2_g, ffn_w_in, ffn_w_out, final_g,
              da_wqkv, da_lambda, da_subln_g, da_wo, sc_w_in, sc_conv_w, sc_w_out,
              wa_wqkv, wa_sinks, wa_wo, hg_w_in, hg_lb, hg_gnorm_g, hg_wo):
    B, L, _ = x.shape
    cos, sin = rope_tables(L)
    cos, sin = cos.astype(x.dtype), sin.astype(x.dtype)
    silu_c = jax.nn.silu(c)
    silu_cc = jax.nn.silu(c_ctx)[None, :]
    for i in range(DEPTH_2):
        mixer, slot = i % N_MIXERS, i // N_MIXERS
        need_ctx = i < DEPTH_2 - 1
        mod = (silu_c @ ada_w[i] + ada_b[i])[:, None, :]
        mod_c = (silu_cc @ ada_w[i] + ada_b[i])[:, None, :]
        sh1, sc1, g1, sh2, sc2, g2 = jnp.split(mod, N_MOD, axis=-1)
        csh1, csc1, cg1, csh2, csc2, cg2 = jnp.split(mod_c, N_MOD, axis=-1)
        h = modulate(rmsnorm_2(x, norm1_g[i]), sh1, sc1)
        hc = modulate(rmsnorm_2(ctx, norm1_g[i]), csh1, csc1)
        if mixer == 0:
            yc, y = diff_attention(h, hc, da_wqkv[slot], da_lambda[slot], da_subln_g[slot],
                                   da_wo[slot], cos, sin, i, need_ctx)
        elif mixer == 1:
            yc, y = short_conv(h, hc, sc_w_in[slot], sc_conv_w[slot], sc_w_out[slot], need_ctx)
        elif mixer == 2:
            yc, y = window_attention(h, hc, wa_wqkv[slot], wa_sinks[slot], wa_wo[slot],
                                     cos, sin, need_ctx)
        else:
            yc, y = hgrn2(h, hc, hg_w_in[slot], hg_lb, hg_gnorm_g[slot], hg_wo[slot], i, need_ctx)
        x = x + g1 * y
        x = x + g2 * swiglu(modulate(rmsnorm_2(x, norm2_g[i]), sh2, sc2), ffn_w_in[i], ffn_w_out[i])
        if need_ctx:
            ctx = ctx + cg1 * yc
            ctx = ctx + cg2 * swiglu(modulate(rmsnorm_2(ctx, norm2_g[i]), csh2, csc2),
                                     ffn_w_in[i], ffn_w_out[i])
    return rmsnorm_2(x, final_g)


def setup_inputs(seed=0):
    out = dict(first_inputs(seed))
    for name, value in second_inputs(seed + 1).items():
        if name != "x":
            out[name + "_2"] = value
    return out


def reference(
    x, mem, norm_mix_g, w_in, gdn_conv_w, gdn_a_log, gdn_dt_bias, gdn_norm_g, gla_w_gate2,
    gla_b_gate, gla_norm_g, w_branch_gdn, w_branch_gla, w_out, norm_xattn_g, norm_mem_g,
    xattn_wq, xattn_wk, xattn_wv, xattn_wo, norm_mlp_g, mlp_w1, mlp_w2, norm_final_g, c_2,
    ctx_2, c_ctx_2, ada_w_2, ada_b_2, norm1_g_2, norm2_g_2, ffn_w_in_2, ffn_w_out_2, final_g_2,
    da_wqkv_2, da_lambda_2, da_subln_g_2, da_wo_2, sc_w_in_2, sc_conv_w_2, sc_w_out_2,
    wa_wqkv_2, wa_sinks_2, wa_wo_2, hg_w_in_2, hg_lb_2, hg_gnorm_g_2, hg_wo_2,
):
    x = first_block(
        x, mem, norm_mix_g, w_in, gdn_conv_w, gdn_a_log, gdn_dt_bias, gdn_norm_g, gla_w_gate2,
        gla_b_gate, gla_norm_g, w_branch_gdn, w_branch_gla, w_out, norm_xattn_g, norm_mem_g,
        xattn_wq, xattn_wk, xattn_wv, xattn_wo, norm_mlp_g, mlp_w1, mlp_w2, norm_final_g,
    )
    return second_block(
        x, c_2, ctx_2, c_ctx_2, ada_w_2, ada_b_2, norm1_g_2, norm2_g_2, ffn_w_in_2, ffn_w_out_2,
        final_g_2, da_wqkv_2, da_lambda_2, da_subln_g_2, da_wo_2, sc_w_in_2, sc_conv_w_2,
        sc_w_out_2, wa_wqkv_2, wa_sinks_2, wa_wo_2, hg_w_in_2, hg_lb_2, hg_gnorm_g_2, hg_wo_2,
    )


_drawn_inputs = setup_inputs


def setup_inputs(seed=0):
    import zlib

    import numpy as np

    out = dict(_drawn_inputs(seed))
    spreads = {}
    factors = {'norm_mix_g': 2.952,
     'gdn_norm_g': 7.192,
     'gla_b_gate': 3.61,
     'gla_norm_g': 7.675,
     'norm_xattn_g': 8.0,
     'norm_mem_g': 8.0,
     'norm_mlp_g': 3.048,
     'norm1_g_2': 4.45,
     'norm2_g_2': 6.603,
     'final_g_2': 2.887,
     'da_lambda_2': 4.571,
     'da_subln_g_2': 8.0}
    for name, (base, spread) in spreads.items():
        noise = np.random.default_rng([zlib.crc32(name.encode()), seed]).standard_normal(out[name].shape)
        drawn = base * np.exp(spread * noise) if base else spread * noise
        out[name] = jnp.asarray(drawn.astype(out[name].dtype))
    for name, factor in factors.items():
        out[name] = (out[name] * factor).astype(out[name].dtype)
    return out
```

```python
from contextlib import ExitStack

import numpy as np
import concourse.bass as bass
from concourse import mybir

F32 = mybir.dt.float32
F32R = mybir.dt.float32r
ACT = mybir.ActivationFunctionType
ALU = mybir.AluOpType
AX = mybir.AxisListType.X

P = 128
D = 1024
DT = D // P
T = 512
MEM = 256
CTX = 256
CHUNK = 128
NCH = T // CHUNK
GDN_H = 8
GLA_H = 4
XA_H = 4
DA_H = 8
F1 = 4096
F2 = 2816
PW = 256
EPS = 1e-6
GLA_TAU = 16.0
LAM_INIT = 0.8 - 0.6 * float(np.exp(-0.3 * 0))

GZ0, GA0, LQ0, LV0, LR0, LG0, GTA0, GTB0 = 3072, 4096, 4112, 5136, 6160, 7184, 7200, 8224

PARAM_WIDTHS = (
    ("norm_mix_g", 8), ("gdn_conv_w", 96), ("a_log", 8), ("dt_bias", 8), ("gdn_norm_g", 1),
    ("gla_b_gate", 4), ("gla_norm_g", 2), ("norm_xattn_g", 8), ("norm_mem_g", 8), ("norm_mlp_g", 8),
    ("norm_final_g", 8),
    ("c", 8), ("c_ctx", 8), ("ada_b0", 48), ("ada_b1", 48), ("norm1_g0", 8), ("norm1_g1", 8),
    ("norm2_g0", 8), ("norm2_g1", 8), ("final_g", 8), ("lam", 4), ("subln_g", 1), ("sc_conv_w", 24),
    ("eps", 1), ("eps4", 1),
)
PARAM_AT = {}
_at = 0
for _name, _width in PARAM_WIDTHS:
    PARAM_AT[_name] = (_at, _width)
    _at += _width
N_PARAMS = _at

CONSTS = ("ident", "ones", "incl_t", "strict", "strict_t", "lvl1", "lvl1_t",
          "lvl2_t", "lvl4_t", "lvl8_t", "lvl16_t", "lvl32_t", "lvl64_t")


def pair_columns(first, second, n):
    return [list(range(first + i * P, first + (i + 1) * P)) + list(range(second + i * P, second + (i + 1) * P))
            for i in range(n)]


def run_columns(start, n, width=PW):
    return [list(range(start + i * width, start + (i + 1) * width)) for i in range(n // width)]


def k_blocks(k):
    return [(t, min(8, k // P - t)) for t in range(0, k // P, 8)]


def panel_plan():
    full = [(0, 8)]
    plan = [
        ("gates", "w_in", full, [list(range(GA0, GA0 + 16)) + list(range(LG0, LG0 + 16))]),
        ("gdn_qkv", "w_in", full, run_columns(0, 3072)),
        ("gdn_z", "w_in", full, run_columns(GZ0, 1024)),
        ("gate_a", "w_in", full, run_columns(GTA0, 1024)),
        ("branch_a", "w_branch_gdn", full, run_columns(0, D)),
        ("gla_qk", "w_in", full, run_columns(LQ0, 1024)),
        ("gla_v", "w_in", full, run_columns(LV0, 1024)),
        ("gla_r", "w_in", full, run_columns(LR0, 1024)),
        ("gate_b", "w_in", full, run_columns(GTB0, 1024)),
        ("branch_b", "w_branch_gla", full, run_columns(0, D)),
        ("w_out", "w_out", full, run_columns(0, D)),
        ("xk", "xattn_wk", full, run_columns(0, D)),
        ("xv", "xattn_wv", full, run_columns(0, D)),
        ("xq", "xattn_wq", full, run_columns(0, D)),
        ("xo", "xattn_wo", full, run_columns(0, D)),
        ("mlp1", "mlp_w1", full, run_columns(0, F1)),
        ("mlp2", "mlp_w2", k_blocks(F1), run_columns(0, D)),
        ("da_k", "da_wqkv_2", full, run_columns(D, D)),
        ("da_v", "da_wqkv_2", full, run_columns(2 * D, D)),
        ("da_q", "da_wqkv_2", full, run_columns(0, D)),
        ("da_o", "da_wo_2", full, run_columns(0, D)),
        ("ffn1_0", "ffn_w_in_2.0", full, pair_columns(0, F2, F2 // P)),
        ("ffn2_0", "ffn_w_out_2.0", k_blocks(F2), run_columns(0, D)),
        ("sc_cu", "sc_w_in_2", full, pair_columns(D, 2 * D, DT)),
        ("sc_b", "sc_w_in_2", full, run_columns(0, D)),
        ("sc_o", "sc_w_out_2", full, run_columns(0, D)),
        ("ffn1_1", "ffn_w_in_2.1", full, pair_columns(0, F2, F2 // P)),
        ("ffn2_1", "ffn_w_out_2.1", k_blocks(F2), run_columns(0, D)),
    ]
    return plan


def build_program(nc, dram, out_t):
    top = ExitStack()

    class Queue:

        def __init__(self, engine, name):
            self.engine, self.items, self.count = engine, [], 0
            self.sem = top.enter_context(nc.semaphore(name))
            self.seen, self.unsignalled = {}, False

        def wait(self, tokens):
            for token in tokens:
                if token is None:
                    continue
                sem, value = token
                if self.seen.get(sem.name, 0) >= value:
                    continue
                self.seen[sem.name] = value
                self.items.append(lambda e, s=sem, v=value: e.wait_ge(s, v))

        def op(self, issue, after=(), signal=True):
            self.wait(after)
            if not signal:
                self.items.append(issue)
                self.unsignalled = True
                return None
            self.count += 1
            self.unsignalled = False
            self.items.append(lambda e: issue(e).then_inc(self.sem, 1))
            return (self.sem, self.count)

        def last(self):
            assert not self.unsignalled
            return (self.sem, self.count) if self.count else None

        def place(self):
            spot = []
            self.items.append(spot)
            return spot

        def flush(self):
            def run(items):
                for item in items:
                    if isinstance(item, list):
                        run(item)
                    else:
                        item(self.engine)
            run(self.items)

    pe, act, dve, pool, sp = (Queue(e, n) for e, n in (
        (nc.tensor, "pe_done"), (nc.scalar, "act_done"), (nc.vector, "dve_done"),
        (nc.gpsimd, "pool_done"), (nc.sync, "sp_done")))
    engines = (pe, act, dve, pool)

    def everything():
        return [q.last() for q in engines]

    def fence():
        marks = everything()
        for q in engines:
            q.wait(marks)

    loads = [0]

    def load(dst, src, after=(), queue=None):
        queue = queue or pool
        sem = top.enter_context(nc.semaphore(f"load{loads[0]}"))
        loads[0] += 1
        queue.wait(after)
        queue.items.append(lambda e: e.dma_start(dst, src).then_inc(sem, 16))
        return (sem, 16)

    def sb(stack, name, shape, dt=F32):
        return stack.enter_context(nc.sbuf_tensor(name, shape, dt))

    x_t = sb(top, "x_t", [P, DT, T])
    h_hi = sb(top, "h_hi", [P, DT, T], F32R)
    h_lo = sb(top, "h_lo", [P, DT, T], F32R)
    N_RAW, N_SPLIT = 3, 2
    w_raw = [sb(top, f"w_raw{i}", [P, DT * PW]) for i in range(N_RAW)]
    w_hi = [sb(top, f"w_hi{i}", [P, DT * PW], F32R) for i in range(N_SPLIT)]
    w_lo = [sb(top, f"w_lo{i}", [P, DT * PW], F32R) for i in range(N_SPLIT)]
    prm = sb(top, "prm", [P, N_PARAMS])
    cst = sb(top, "cst", [P, len(CONSTS), P])
    mod = sb(top, "mod", [P, 112])
    rstd = sb(top, "rstd", [P, T])
    lam_col = sb(top, "lam_col", [P, 4])
    banks = [top.enter_context(nc.psum_tensor(f"bank{i}", [P, 512], F32)) for i in range(8)]

    def param(name, a=0, b=None):
        at, width = PARAM_AT[name]
        return prm[:, at + a:at + (width if b is None else b)]

    def const(name):
        return cst[:, CONSTS.index(name), :]

    class Ring:

        def __init__(self, buffers):
            self.buffers, self.free, self.n = buffers, [()] * len(buffers), 0

        def take(self):
            i = self.n % len(self.buffers)
            self.n += 1
            return i, self.buffers[i], self.free[i]

        def give(self, i, *readers):
            self.free[i] = readers

    gemm_banks = Ring(banks[0:4])
    work_banks = Ring(banks[4:8])

    raw_loaded = [top.enter_context(nc.semaphore(f"raw_loaded{i}")) for i in range(N_RAW)]
    hi_made = top.enter_context(nc.semaphore("hi_made"))
    lo_made = top.enter_context(nc.semaphore("lo_made"))

    plan, offset, where = panel_plan(), {}, {}
    for key, weight, blocks, columns in plan:
        where[key] = []
        offset.setdefault(key, 0)
        at = 0
        for k0, nk in blocks:
            row = []
            for cols in columns:
                row.append((at, nk, len(cols)))
                at += P * nk * len(cols)
            where[key].append(row)
    panel_n = [0]
    panel_end = []
    spots = {}

    def leave_spot():
        n = panel_n[0]
        spots[n] = (sp.place(), act.place(), dve.place())

    def panel(key, block, i):
        n = panel_n[0]
        at, nk, width = where[key][block][i]
        size = nk * width
        raw, raw_sem, raw_n = w_raw[n % N_RAW], raw_loaded[n % N_RAW], n // N_RAW + 1
        hi, lo = w_hi[n % N_SPLIT], w_lo[n % N_SPLIT]
        sp_spot, act_spot, dve_spot = spots.pop(n)
        if n >= N_RAW:
            sp_spot.append(lambda e: e.wait_ge(lo_made, n - N_RAW + 1))
        src = dram["pack_" + key][at:at + P * size].rearrange("(p f) -> p f", p=P)
        sp_spot.append(lambda e: e.dma_start(raw[:, 0:size], src).then_inc(raw_sem, 16))
        act_spot.append(lambda e: e.wait_ge(raw_sem, 16 * raw_n))
        if n >= N_SPLIT:
            used = panel_end[n - N_SPLIT]
            act_spot.append(lambda e: e.wait_ge(*used))
        act_spot.append(lambda e: e.activation(hi[:, 0:size], raw[:, 0:size], ACT.Copy).then_inc(hi_made, 1))
        dve_spot.append(lambda e: e.wait_ge(hi_made, n + 1))
        dve_spot.append(lambda e: e.tensor_tensor(
            lo[:, 0:size], raw[:, 0:size], hi[:, 0:size].bitcast(F32), ALU.subtract).then_inc(lo_made, 1))
        panel_n[0] += 1
        leave_spot()
        pe.items.append(lambda e: e.wait_ge(lo_made, n + 1))
        view = lambda t: t[:, 0:size].rearrange("p (k n) -> p k n", k=nk)
        return view(hi), view(lo), nk, width

    def end_panel():
        panel_end.append(pe.last())
        return pe.last()

    def products(out, pairs, after=(), signal=True):
        pe.wait(after)
        todo = []
        for (lh, ll), (rh, rl) in pairs:
            todo += [(lh, rh), (lh, rl), (ll, rh)]
        token = None
        for n, (a, b) in enumerate(todo):
            last = n == len(todo) - 1
            issue = lambda e, a=a, b=b, n=n, last=last: e.matmul(out, a, b, start=(n == 0), stop=last)
            token = pe.op(issue, signal=signal and last)
        return token

    def mm(out, lhs, rhs, start=True, stop=True, after=(), signal=True):
        return pe.op(lambda e: e.matmul(out, lhs, rhs, start=start, stop=stop), after, signal)

    def transpose(out, in_, after=(), signal=True):
        return pe.op(lambda e: e.transpose(out, in_, const("ident")), after, signal)

    def split(hi, lo, src, after):
        a = act.op(lambda e: e.activation(hi, src, ACT.Copy), after)
        b = dve.op(lambda e: e.tensor_tensor(lo, src, hi.bitcast(F32), ALU.subtract), [a])
        return b

    def gemm(key, block, act_hi, act_lo, tokens, ready, evacuate, token_major=False):
        for i in range(len(where[key][block])):
            hi, lo, nk, width = panel(key, block, i)
            if token_major:
                for m in range(tokens // P):
                    b, bank, free = gemm_banks.take()
                    pe.wait(list(free) + [ready(k) for k in range(nk)])
                    cut = slice(m * P, (m + 1) * P)
                    tok = products(bank[:, 0:width], [((act_hi[:, k, cut], act_lo[:, k, cut]),
                                                       (hi[:, k, :], lo[:, k, :])) for k in range(nk)])
                    if m == tokens // P - 1:
                        tok = end_panel()
                    gemm_banks.give(b, *evacuate(i, m, bank[:, 0:width], tok))
                continue
            for c in range(width // P):
                b, bank, free = gemm_banks.take()
                pe.wait(list(free) + [ready(k) for k in range(nk)])
                cut = slice(c * P, (c + 1) * P)
                tok = products(bank[:, 0:tokens], [((hi[:, k, cut], lo[:, k, cut]),
                                                   (act_hi[:, k, 0:tokens], act_lo[:, k, 0:tokens]))
                                                  for k in range(nk)])
                if c == width // P - 1:
                    tok = end_panel()
                gemm_banks.give(b, *evacuate(i * (PW // P) + c, bank[:, 0:tokens], tok))

    got_prm = load(prm[:, :], dram["params"], queue=act)
    got_cst = load(cst[:, :, :], dram["consts"].rearrange("p (n f) -> p n f", n=len(CONSTS)), queue=act)
    got_x = load(x_t[:, :, :], dram["x_t"].rearrange("(k p) t -> p k t", p=P), queue=act)
    for q in engines:
        q.wait([got_prm, got_cst, got_x])
    leave_spot()

    def rms_stats(stack, name, src, n_tiles, tokens, count, eps="eps", scale=None):
        sq = [sb(stack, f"{name}_sq{i}", [P, tokens]) for i in range(2)]
        ring = Ring(sq)
        b, bank, free = work_banks.take()
        tok = None
        for k in range(n_tiles):
            i, buf, rd = ring.take()
            s = act.op(lambda e, k=k, buf=buf: e.activation(buf[:, :], src(k), ACT.Square), rd)
            tok = mm(bank[:, 0:tokens], const("ones"), buf[:, :], start=(k == 0), stop=(k == n_tiles - 1),
                     after=[s] + list(free))
            ring.give(i, tok)
        a = act.op(lambda e: e.activation(rstd[:, 0:tokens], bank[:, 0:tokens], ACT.Sqrt,
                                          bias=param(eps), scale=1.0 / count), [tok])
        work_banks.give(b, a)
        return dve.op(lambda e: e.reciprocal(rstd[:, 0:tokens], rstd[:, 0:tokens]), [a])

    def norm_to_h(stack, name, src, gain, shift, tokens, hi, lo):
        fence()
        r = rms_stats(stack, name, src, DT, tokens, D)
        tmp = Ring([sb(stack, f"{name}_y{i}", [P, tokens]) for i in range(2)])
        toks = []
        for k in range(DT):
            i, y, rd = tmp.take()
            t = dve.op(lambda e, k=k, y=y: e.scalar_tensor_tensor(
                out=y[:, :], in0=src(k), scalar=gain(k), in1=rstd[:, 0:tokens],
                op0=ALU.mult, op1=ALU.mult), list(rd) + [r])
            if shift is not None:
                t = dve.op(lambda e, k=k, y=y: e.tensor_scalar(y[:, :], y[:, :], shift(k), None, ALU.add), [t])
            t = split(hi[:, k, 0:tokens], lo[:, k, 0:tokens], y[:, :], [t])
            tmp.give(i, t)
            toks.append(t)
        return toks

    def mixer():
        outer = ExitStack()
        with ExitStack() as st:
            h_ready = norm_to_h(st, "mix", lambda k: x_t[:, k, :], lambda k: param("norm_mix_g", k, k + 1),
                                None, T, h_hi, h_lo)
            fence()
        ready = lambda k: h_ready[k]
        lgate = sb(outer, "lgate", [16, T])
        o_t = sb(outer, "heads_t", [P, DT, T])
        with ExitStack() as st2:
            gdn(st2, o_t, ready, lgate)
            fence()
        merged = sb(outer, "merged", [P, DT, T])
        with ExitStack() as st:
            o_hi = sb(st, "oa_hi", [P, DT, T], F32R)
            o_lo = sb(st, "oa_lo", [P, DT, T], F32R)
            gated_norm(st, "oa", o_t, 1, GDN_H, "gdn_norm_g", "gdn_z", ready, o_hi, o_lo)
            gate_and_branch(st, "a", "gate_a", "branch_a", ready, o_hi, o_lo, merged, True)
            fence()
        with ExitStack() as st:
            with ExitStack() as st2:
                gla(st2, o_t, ready, lgate)
                fence()
            o_hi = sb(st, "ob_hi", [P, DT, T], F32R)
            o_lo = sb(st, "ob_lo", [P, DT, T], F32R)
            gated_norm(st, "ob", o_t, 2, GLA_H, "gla_norm_g", "gla_r", ready, o_hi, o_lo)
            gate_and_branch(st, "b", "gate_b", "branch_b", ready, o_hi, o_lo, merged, False)
            fence()
        m_ready = []
        for k in range(DT):
            t = dve.op(lambda e, k=k: e.tensor_scalar(merged[:, k, :], merged[:, k, :], 0.5, None, ALU.mult))
            m_ready.append(split(h_hi[:, k, :], h_lo[:, k, :], merged[:, k, :], [t]))
        gemm("w_out", 0, h_hi, h_lo, T, lambda k: m_ready[k], add_to_x)
        fence()
        outer.close()

    def add_to_x(n, ps, tok):
        return [dve.op(lambda e: e.tensor_tensor(x_t[:, n, :], x_t[:, n, :], ps, ALU.add), [tok])]

    def gated_norm(st, name, o, tiles, heads, gain, key, ready, o_hi, o_lo):
        sq = Ring([sb(st, f"{name}_hsq{i}", [P, T]) for i in range(2)])
        normed = []
        for h in range(heads):
            b, bank, free = work_banks.take()
            for j in range(tiles):
                i, buf, rd = sq.take()
                s = act.op(lambda e, k=h * tiles + j, buf=buf: e.activation(buf[:, :], o[:, k, :], ACT.Square), rd)
                tok = mm(bank[:, :], const("ones"), buf[:, :], start=(j == 0), stop=(j == tiles - 1),
                         after=[s] + list(free))
                sq.give(i, tok)
            i, r, rd = sq.take()
            a = act.op(lambda e, r=r, bank=bank: e.activation(r[:, :], bank[:, :], ACT.Sqrt, bias=param("eps"),
                                                              scale=1.0 / (P * tiles)), [tok] + list(rd))
            work_banks.give(b, a)
            t = dve.op(lambda e, r=r: e.reciprocal(r[:, :], r[:, :]), [a])
            for j in range(tiles):
                k = h * tiles + j
                t2 = dve.op(lambda e, k=k, j=j, r=r: e.scalar_tensor_tensor(
                    out=o[:, k, :], in0=o[:, k, :], scalar=param(gain, j, j + 1), in1=r[:, :],
                    op0=ALU.mult, op1=ALU.mult), [t])
                normed.append(t2)
            sq.give(i, t2)
        tmp = Ring([sb(st, f"{name}_z{i}", [P, T]) for i in range(2)])
        done = {}

        def take_z(n, ps, tok):
            i, z, rd = tmp.take()
            a = act.op(lambda e: e.activation(z[:, :], ps, ACT.Tanh, scale=0.5), [tok] + list(rd))
            t = dve.op(lambda e: e.scalar_tensor_tensor(out=z[:, :], in0=z[:, :], scalar=1.0, in1=ps,
                                                        op0=ALU.add, op1=ALU.mult), [a])
            t2 = dve.op(lambda e: e.scalar_tensor_tensor(out=z[:, :], in0=z[:, :], scalar=0.5, in1=o[:, n, :],
                                                         op0=ALU.mult, op1=ALU.mult), [t, normed[n]])
            done[n] = split(o_hi[:, n, :], o_lo[:, n, :], z[:, :], [t2])
            tmp.give(i, done[n])
            return [t]

        gemm(key, 0, h_hi, h_lo, T, ready, take_z)
        o_ready.clear()
        o_ready.update(done)

    o_ready = {}

    def gate_and_branch(st, name, gate_key, branch_key, ready, o_hi, o_lo, merged, first):
        g = sb(st, f"gate_{name}", [P, DT, T])
        g_ready = {}

        def take_gate(n, ps, tok):
            g_ready[n] = act.op(lambda e: e.activation(g[:, n, :], ps, ACT.Tanh, scale=0.5), [tok])
            return [g_ready[n]]

        gemm(gate_key, 0, h_hi, h_lo, T, ready, take_gate)
        branch_ready = dict(o_ready)

        def take_branch(n, ps, tok):
            dst = merged[:, n, :] if first else g[:, n, :]
            t = dve.op(lambda e: e.scalar_tensor_tensor(out=dst, in0=g[:, n, :], scalar=1.0, in1=ps,
                                                        op0=ALU.add, op1=ALU.mult), [tok, g_ready[n]])
            if not first:
                dve.op(lambda e: e.tensor_tensor(merged[:, n, :], merged[:, n, :], g[:, n, :], ALU.add), [t])
            return [t]

        gemm(branch_key, 0, o_hi, o_lo, T, lambda k: branch_ready[k], take_branch)

    def softplus_parts(st, name, z, shape, ready):
        a = sb(st, f"{name}_abs", shape)
        flat = a[:, :]
        t = act.op(lambda e: e.activation(flat, z, ACT.Abs), [ready])
        t = act.op(lambda e: e.activation(flat, flat, ACT.Exp, scale=-1.0), [t])
        t = act.op(lambda e: e.activation(flat, flat, ACT.Ln, bias=1.0), [t])
        return a, t

    def gdn(st, q_t, ready, lgate):
        k_t = sb(st, "k_t", [P, GDN_H, T])
        v_t = sb(st, "v_t", [P, GDN_H, T])
        gb = sb(st, "gdn_gb", [P, NCH * 16])
        gbv = gb[:, :].rearrange("p (c n) -> p c n", c=NCH)
        beta = sb(st, "beta", [P, NCH * 8])
        g = sb(st, "gdn_g", [P, NCH * 8])
        z = sb(st, "gdn_zg", [P, NCH * 8])
        neg_a = sb(st, "neg_a", [P, 8])

        hi, lo, nk, width = panel("gates", 0, 0)
        toks = []
        b, bank, free = gemm_banks.take()
        for c in range(NCH):
            cut = slice(c * P, (c + 1) * P)
            t = products(bank[:, c * 16:(c + 1) * 16],
                         [((h_hi[:, k, cut], h_lo[:, k, cut]), (hi[:, k, 0:16], lo[:, k, 0:16])) for k in range(nk)],
                         after=list(free) + [ready(k) for k in range(nk)])
        t = act.op(lambda e, bank=bank: e.activation(gb[:, :], bank[:, 0:NCH * 16], ACT.Copy), [t])
        gemm_banks.give(b, t)
        b, bank, free = gemm_banks.take()
        products(bank[0:16, :], [((hi[:, k, 16:32], lo[:, k, 16:32]), (h_hi[:, k, :], h_lo[:, k, :]))
                                 for k in range(nk)], after=free)
        tl = end_panel()
        tl = act.op(lambda e, bank=bank: e.activation(lgate[:, :], bank[0:16, :], ACT.Copy), [tl])
        gemm_banks.give(b, tl)

        v3 = lambda tile: tile[:, :].rearrange("p (c n) -> p c n", c=NCH)
        bc = lambda ap: ap[:, None, :].to_broadcast([P, NCH, 8])
        tb = act.op(lambda e: e.activation(v3(beta), gbv[:, :, 8:16], ACT.Tanh, scale=0.5), [t])
        tb = dve.op(lambda e: e.tensor_scalar(beta[:, :], beta[:, :], 0.5, 0.5, ALU.mult, ALU.add), [tb])
        tz = dve.op(lambda e: e.tensor_tensor(v3(z), gbv[:, :, 0:8], bc(param("dt_bias")), ALU.add), [t])
        ta = act.op(lambda e: e.activation(neg_a[:, :], param("a_log"), ACT.Exp))
        sp_tile, ts = softplus_parts(st, "gdn_sp", z[:, :], [P, NCH * 8], tz)
        tz = dve.op(lambda e: e.scalar_tensor_tensor(out=z[:, :], in0=z[:, :], scalar=0.0, in1=sp_tile[:, :],
                                                     op0=ALU.max, op1=ALU.add), [ts])
        tz = dve.op(lambda e: e.scalar_tensor_tensor(out=v3(g), in0=v3(z), scalar=-1.0, in1=bc(neg_a[:, :]),
                                                     op0=ALU.mult, op1=ALU.mult), [tz, ta])
        g_ready = tz

        with ExitStack() as cs:
            raws = [sb(cs, f"conv_in{i}", [P, T + 4]) for i in range(2)]
            pads = [pool.op(lambda e, r=r: e.memset(r[:, 0:3], 0.0)) for r in raws]
            raw_ring = Ring(raws)
            raw_ring.free = [(p,) for p in pads]
            tanhs = Ring([sb(cs, f"conv_tanh{i}", [P, T]) for i in range(2)])
            made = {}

            def conv(n, ps, tok):
                i, raw, rd = raw_ring.take()
                a = act.op(lambda e: e.activation(raw[:, 3:3 + T], ps, ACT.Copy), [tok] + list(rd))
                dst = (q_t, k_t, v_t)[n // GDN_H][:, n % GDN_H, :]
                w = lambda j: param("gdn_conv_w", n * 4 + j, n * 4 + j + 1)
                t = dve.op(lambda e: e.tensor_scalar(dst, raw[:, 0:T], w(0), None, ALU.mult), [a])
                for j in range(1, 4):
                    t = dve.op(lambda e, j=j: e.scalar_tensor_tensor(
                        out=dst, in0=raw[:, j:j + T], scalar=w(j), in1=dst, op0=ALU.mult, op1=ALU.add), [t])
                raw_ring.give(i, t)
                i2, th, rd2 = tanhs.take()
                s = act.op(lambda e: e.activation(th[:, :], dst, ACT.Tanh, scale=0.5), [t] + list(rd2))
                t = dve.op(lambda e: e.scalar_tensor_tensor(out=dst, in0=th[:, :], scalar=1.0, in1=dst,
                                                            op0=ALU.add, op1=ALU.mult), [s])
                tanhs.give(i2, t)
                made[n] = t
                return [a]

            gemm("gdn_qkv", 0, h_hi, h_lo, T, ready, conv)
            for n in range(2 * GDN_H):
                tile = (q_t, k_t)[n // GDN_H][:, n % GDN_H, :]
                i, sqb, rd = tanhs.take()
                s = act.op(lambda e, tile=tile, sqb=sqb: e.activation(sqb[:, :], tile, ACT.Square),
                           [made[n]] + list(rd))
                b, bank, free = work_banks.take()
                tok = mm(bank[:, :], const("ones"), sqb[:, :], after=[s] + list(free))
                s = act.op(lambda e, sqb=sqb, bank=bank: e.activation(sqb[:, :], bank[:, :], ACT.Sqrt,
                                                                      bias=param("eps4")), [tok])
                work_banks.give(b, s)
                t = dve.op(lambda e, sqb=sqb: e.reciprocal(sqb[:, :], sqb[:, :]), [s])
                scale = P ** -0.5 if n < GDN_H else 1.0
                t = dve.op(lambda e, tile=tile, sqb=sqb, scale=scale: e.scalar_tensor_tensor(
                    out=tile, in0=tile, scalar=scale, in1=sqb[:, :], op0=ALU.mult, op1=ALU.mult), [t])
                tanhs.give(i, t)
            fence()

        W4 = [P, 4, P]

        def t4(name):
            return sb(st, name, W4)

        g_u, e_row, e_mat, e_mat_t, low, low_t, dd, dd_t, pp, off_t = (
            [t4(f"{n}_{i}") for i in range(1)][0] for n, i in
            (("g_u", 0), ("e_row", 0), ("e_mat", 0), ("e_mat_t", 0), ("low", 0), ("low_t", 0),
             ("dd", 0), ("dd_t", 0), ("pp", 0), ("off_t", 0)))
        kb = t4("kb")
        a_t = t4("a_t")
        state = sb(st, "gdn_state", [P, GDN_H, P])
        cols = sb(st, "gdn_cols", [P, 4, 8])
        b_v, kbg, kdec, w_t, u_m, delta, q_dec = e_mat, low, off_t, pp, low_t, dd, g_u
        gv = v3(g)
        bv3 = v3(beta)
        flat = lambda ap: ap.rearrange("p a b -> p (a b)")
        bank4 = lambda bank: bank[:, :].rearrange("p (h f) -> p h f", h=4)
        mask4 = lambda name: const(name)[:, None, :].to_broadcast(W4)

        def all_last():
            return [q.last() for q in (pe, act, dve, pool)]

        for c in range(NCH):
            tok_cut = slice(c * P, (c + 1) * P)
            b, bank, free = work_banks.take()
            mm(bank[:, 0:8], const("incl_t"), gv[:, c, :], after=list(free) + [g_ready], signal=False)
            t = mm(bank[:, 8:16], const("strict"), gv[:, c, :])
            t = act.op(lambda e, bank=bank: e.activation(cols[:, 0:2, :], bank[:, 0:16].rearrange(
                "p (a h) -> p a h", a=2), ACT.Exp), [t] + all_last())
            work_banks.give(b, t)
            t = dve.op(lambda e, c=c: e.tensor_tensor(cols[:, 2, :], cols[:, 0, :], bv3[:, c, :], ALU.mult), [t])
            t_cols = dve.op(lambda e, c=c: e.tensor_scalar(cols[:, 3, :], bv3[:, c, :], 0.5, None, ALU.mult), [t])
            for grp in range(2):
                hs = slice(4 * grp, 4 * grp + 4)
                col4 = lambda r, grp=grp: cols[:, r, 4 * grp:4 * grp + 4][:, :, None].to_broadcast(W4)
                barrier = all_last()
                t = dve.op(lambda e, c=c, grp=grp: e.tensor_tensor(
                    g_u[:, :, :], mask4("incl_t"),
                    gv[:, c, 4 * grp:4 * grp + 4][:, :, None].to_broadcast(W4), ALU.mult), barrier)
                t_gu = t
                b, bank, free = work_banks.take()
                t = mm(bank[:, :], const("ones"), flat(g_u[:, :, :]), after=[t_gu] + list(free))
                t_er = act.op(lambda e, bank=bank: e.activation(flat(e_row[:, :, :]), bank[:, :], ACT.Exp), [t])
                work_banks.give(b, t_er)
                b, bank, free = work_banks.take()
                for h in range(4):
                    t = mm(bank4(bank)[:, h, :], g_u[:, h, :], const("strict"), after=free, signal=(h == 3))
                t_e = act.op(lambda e, bank=bank: e.activation(flat(e_mat[:, :, :]), bank[:, :], ACT.Exp), [t])
                work_banks.give(b, t_e)
                b, bank, free = work_banks.take()
                t_gu_read = mm(bank[:, :], const("strict"), flat(g_u[:, :, :]), after=free)
                t_et = act.op(lambda e, bank=bank: e.activation(flat(e_mat_t[:, :, :]), bank[:, :], ACT.Exp),
                              [t_gu_read])
                work_banks.give(b, t_et)
                t = dve.op(lambda e, c=c, grp=grp: e.tensor_tensor(
                    pp[:, :, :], mask4("ident"),
                    bv3[:, c, 4 * grp:4 * grp + 4][:, :, None].to_broadcast(W4), ALU.mult))
                b, bank, free = work_banks.take()
                t = mm(bank[:, :], const("ones"), flat(pp[:, :, :]), after=[t] + list(free))
                t_kb = dve.op(lambda e, bank=bank, hs=hs, cut=tok_cut: e.tensor_tensor(
                    kb[:, :, :], k_t[:, hs, cut], bank4(bank), ALU.mult), [t])
                work_banks.give(b, t_kb)
                t_qd = None
                b, bank, free = work_banks.take()
                for h in range(4):
                    t = mm(bank4(bank)[:, h, :], kb[:, h, :], k_t[:, 4 * grp + h, tok_cut],
                           after=[t_kb] + list(free), signal=(h == 3))
                tm = pool.op(lambda e: e.tensor_tensor(e_mat[:, :, :], e_mat[:, :, :], mask4("strict"), ALU.mult),
                             [t_e])
                t_low = dve.op(lambda e, bank=bank: e.tensor_tensor(flat(low[:, :, :]), flat(e_mat[:, :, :]),
                                                                    bank[:, :], ALU.mult), [t, tm])
                work_banks.give(b, t_low)
                b, bank, free = work_banks.take()
                for h in range(4):
                    t = mm(bank4(bank)[:, h, :], k_t[:, 4 * grp + h, tok_cut], kb[:, h, :], after=free,
                           signal=(h == 3))
                tm = pool.op(lambda e: e.tensor_tensor(low_t[:, :, :], e_mat_t[:, :, :], mask4("strict_t"), ALU.mult),
                             [t_et])
                t_lt = dve.op(lambda e, bank=bank: e.tensor_tensor(flat(low_t[:, :, :]), flat(low_t[:, :, :]),
                                                                   bank[:, :], ALU.mult), [t, tm])
                work_banks.give(b, t_lt)
                b, bank, free = work_banks.take()
                for h in range(4):
                    t = mm(bank4(bank)[:, h, :], k_t[:, 4 * grp + h, tok_cut], q_t[:, 4 * grp + h, tok_cut],
                           after=free, signal=(h == 3))
                tm = pool.op(lambda e: e.tensor_tensor(e_mat_t[:, :, :], e_mat_t[:, :, :], mask4("incl_t"), ALU.mult),
                             [tm])
                t_a = dve.op(lambda e, bank=bank: e.tensor_tensor(flat(a_t[:, :, :]), flat(e_mat_t[:, :, :]),
                                                                  bank[:, :], ALU.mult), [t, tm])
                work_banks.give(b, t_a)
                t_qd = pool.op(lambda e, hs=hs, cut=tok_cut: e.tensor_tensor(
                    q_dec[:, :, :], q_t[:, hs, cut], e_row[:, :, :], ALU.mult), [t_er, t_gu_read, t_a])

                t = pool.op(lambda e: e.tensor_tensor(dd[:, :, :], low[:, :, :], mask4("lvl1"), ALU.mult), [t_low])
                t_d = dve.op(lambda e: e.tensor_tensor(dd[:, :, :], mask4("ident"), dd[:, :, :], ALU.subtract), [t])
                t = pool.op(lambda e: e.tensor_tensor(dd_t[:, :, :], low_t[:, :, :], mask4("lvl1_t"), ALU.mult),
                            [t_lt])
                t_dt = dve.op(lambda e: e.tensor_tensor(dd_t[:, :, :], mask4("ident"), dd_t[:, :, :], ALU.subtract),
                              [t])
                t_p_read = None
                for s in (2, 4, 8, 16, 32, 64):
                    t_o = pool.op(lambda e, s=s: e.tensor_tensor(off_t[:, :, :], low_t[:, :, :],
                                                                 mask4(f"lvl{s}_t"), ALU.mult), [t_lt, t_p_read])
                    b, bank, free = work_banks.take()
                    for h in range(4):
                        t = mm(bank4(bank)[:, h, :], off_t[:, h, :], dd[:, h, :], after=[t_o, t_d] + list(free),
                               signal=(h == 3))
                    t_p_read = t
                    t_p = act.op(lambda e, bank=bank: e.activation(flat(pp[:, :, :]), bank[:, :], ACT.Copy), [t])
                    work_banks.give(b, t_p)
                    if s < 64:
                        b, bank, free = work_banks.take()
                        for h in range(4):
                            t = mm(bank4(bank)[:, h, :], dd_t[:, h, :], pp[:, h, :], after=[t_p, t_dt] + list(free),
                                   signal=(h == 3))
                        t_d = dve.op(lambda e, bank=bank: e.tensor_tensor(
                            flat(dd[:, :, :]), flat(dd[:, :, :]), bank[:, :], ALU.subtract), [t])
                        work_banks.give(b, t_d)
                    b, bank, free = work_banks.take()
                    for h in range(4):
                        t = mm(bank4(bank)[:, h, :], pp[:, h, :], dd_t[:, h, :], after=[t_p, t_dt] + list(free),
                               signal=(h == 3))
                    t_dt = dve.op(lambda e, bank=bank: e.tensor_tensor(
                        flat(dd_t[:, :, :]), flat(dd_t[:, :, :]), bank[:, :], ALU.subtract), [t])
                    work_banks.give(b, t_dt)

                b, bank, free = work_banks.take()
                for h in range(4):
                    t = transpose(bank4(bank)[:, h, :], k_t[:, 4 * grp + h, tok_cut], after=free, signal=(h == 3))
                t_kbg = dve.op(lambda e, bank=bank, col4=col4: e.tensor_tensor(
                    kbg[:, :, :], bank4(bank), col4(2), ALU.mult), [t, t_low, t_cols, t_dt])
                t_kd = dve.op(lambda e, bank=bank, col4=col4: e.tensor_tensor(
                    kdec[:, :, :], bank4(bank), col4(1), ALU.mult), [t_kbg])
                work_banks.give(b, t_kd)
                b, bank, free = work_banks.take()
                for h in range(4):
                    t = transpose(bank4(bank)[:, h, :], v_t[:, 4 * grp + h, tok_cut], after=free, signal=(h == 3))
                t_bv = dve.op(lambda e, bank=bank, col4=col4: e.tensor_tensor(
                    b_v[:, :, :], bank4(bank), col4(3), ALU.mult), [t, t_low])
                work_banks.give(b, t_bv)
                b, bank, free = work_banks.take()
                for h in range(4):
                    t = mm(bank4(bank)[:, h, :], dd_t[:, h, :], b_v[:, h, :], after=[t_bv, t_dt] + list(free),
                           signal=(h == 3))
                t_u = act.op(lambda e, bank=bank: e.activation(flat(u_m[:, :, :]), bank[:, :], ACT.Copy), [t])
                work_banks.give(b, t_u)
                if c == 0:
                    delta_now, t_del = u_m, t_u
                else:
                    b, bank, free = work_banks.take()
                    for h in range(4):
                        t = mm(bank4(bank)[:, h, :], kbg[:, h, :], dd_t[:, h, :], after=[t_kbg] + list(free),
                               signal=(h == 3))
                    t_w = act.op(lambda e, bank=bank: e.activation(flat(w_t[:, :, :]), bank[:, :], ACT.Copy), [t])
                    work_banks.give(b, t_w)
                    b, bank, free = work_banks.take()
                    for h in range(4):
                        t = mm(bank4(bank)[:, h, :], w_t[:, h, :], state[:, 4 * grp + h, :],
                               after=[t_w] + list(free), signal=(h == 3))
                    t_del = dve.op(lambda e, bank=bank: e.tensor_tensor(
                        flat(delta[:, :, :]), flat(u_m[:, :, :]), bank[:, :], ALU.subtract), [t, t_u, t_d])
                    work_banks.give(b, t_del)
                    delta_now = delta
                b, bank, free = work_banks.take()
                for h in range(4):
                    if c > 0:
                        mm(bank4(bank)[:, h, :], state[:, 4 * grp + h, :], q_dec[:, h, :], stop=False,
                           after=[t_qd] + list(free), signal=False)
                    t = mm(bank4(bank)[:, h, :], delta_now[:, h, :], a_t[:, h, :], start=(c == 0),
                           after=[t_del, t_a, t_qd] + list(free), signal=(h == 3))
                t_o = act.op(lambda e, bank=bank, hs=hs, cut=tok_cut: e.activation(
                    q_t[:, hs, cut], bank4(bank), ACT.Copy), [t])
                work_banks.give(b, t_o)
                if c < NCH - 1:
                    b, bank, free = work_banks.take()
                    for h in range(4):
                        t = mm(bank4(bank)[:, h, :], kdec[:, h, :], delta_now[:, h, :], after=[t_kd] + list(free),
                               signal=(h == 3))
                    if c == 0:
                        t = act.op(lambda e, bank=bank, hs=hs: e.activation(state[:, hs, :], bank4(bank), ACT.Copy),
                                   [t])
                    else:
                        ts = dve.op(lambda e, hs=hs: e.tensor_tensor(
                            state[:, hs, :], state[:, hs, :], e_row[:, :, P - 1:P].to_broadcast(W4), ALU.mult), [t])
                        t = dve.op(lambda e, bank=bank, hs=hs: e.tensor_tensor(
                            state[:, hs, :], state[:, hs, :], bank4(bank), ALU.add), [ts])
                    work_banks.give(b, t)

    def gla(st, o_t, ready, lgate):
        q = sb(st, "gla_q", [P, GLA_H, T])
        k = sb(st, "gla_k", [P, GLA_H, T])
        v = sb(st, "gla_v", [P, NCH, D])
        w2 = sb(st, "gla_w2", [16, 512])
        bc_sum = sb(st, "gla_bc", [P, T])
        lf = sb(st, "gla_lf", [P, T])
        e_q, kd = q, k
        q_in = sb(st, "gla_qin", [P, T])
        k_in = sb(st, "gla_kin", [P, T])
        k_x = sb(st, "gla_kx", [P, NCH, 64])
        q_x = sb(st, "gla_qx", [P, NCH, 64])
        reset = sb(st, "gla_reset", [P, T])
        a_t = sb(st, "gla_at", [P, NCH, P])
        g_end = sb(st, "gla_gend", [P, GLA_H, NCH])
        t_w2 = load(w2[:, :], dram["gla_w2"], after=everything())
        r4 = reset[:, :].rearrange("p (c i) -> p c i", c=NCH)
        t_rs = pool.op(lambda e: e.memset(reset[:, :], 1.0))
        t_rs = pool.op(lambda e: e.memset(r4[:, :, 0:1], 0.0), [t_rs])
        t_az = pool.op(lambda e: e.memset(a_t[:, :, :], 0.0))
        made = {}

        def take_qk(n, ps, tok):
            dst = q[:, n, :] if n < GLA_H else k[:, n - GLA_H, :]
            made[n] = act.op(lambda e: e.activation(dst, ps, ACT.Copy, scale=P ** -0.5 if n < GLA_H else 1.0), [tok])
            return [made[n]]

        gemm("gla_qk", 0, h_hi, h_lo, T, ready, take_qk)

        def take_v(i, m, ps, tok):
            t = act.op(lambda e: e.activation(v[:, m, i * PW:(i + 1) * PW], ps, ACT.Copy), [tok])
            return [t]

        gemm("gla_v", 0, h_hi, h_lo, T, ready, take_v, token_major=True)
        t_v = act.last()

        c4 = lambda ap: ap.rearrange("p (c i) -> p c i", c=NCH)
        c8 = lambda ap: ap.rearrange("p (c i) -> p c i", c=2 * NCH)
        with ExitStack() as es:
            ex = sb(es, "gla_ex", [P, T])
            ab = sb(es, "gla_ab", [P, T])
            for h in range(GLA_H):
                b, bank, free = work_banks.take()
                t = mm(bank[:, :], w2[:, h * P:(h + 1) * P], lgate[:, :], after=[t_w2] + list(free))
                t = act.op(lambda e, bank=bank, h=h: e.activation(lf[:, :], bank[:, :], ACT.Identity,
                                                                  bias=param("gla_b_gate", h, h + 1)),
                           [t, dve.last()])
                work_banks.give(b, t)
                t = act.op(lambda e: e.activation(ab[:, :], lf[:, :], ACT.Abs), [t])
                t = act.op(lambda e: e.activation(ab[:, :], ab[:, :], ACT.Exp, scale=-1.0), [t])
                t = act.op(lambda e: e.activation(ab[:, :], ab[:, :], ACT.Ln, bias=1.0), [t])
                t = dve.op(lambda e: e.scalar_tensor_tensor(out=lf[:, :], in0=lf[:, :], scalar=0.0, in1=ab[:, :],
                                                            op0=ALU.min, op1=ALU.subtract), [t])
                t = dve.op(lambda e: e.tensor_scalar(lf[:, :], lf[:, :], 1.0 / GLA_TAU, None, ALU.mult), [t])
                t_bc = dve.op(lambda e: e.tensor_tensor_scan(bc_sum[:, :], reset[:, :], lf[:, :], 0.0,
                                                             ALU.mult, ALU.add), [t, t_rs])

                def decayed(dst, src, a, b_, shape, after):
                    exv = ex[:, 0:shape[1] * shape[2]].rearrange("p (c i) -> p c i", c=shape[1])
                    t = dve.op(lambda e: e.tensor_tensor(exv, a, b_, ALU.subtract), list(after) + [dve.last()])
                    t = act.op(lambda e: e.activation(exv, exv, ACT.Exp), [t])
                    return dve.op(lambda e: e.tensor_tensor(dst, src, exv, ALU.mult), [t])

                prev = [pe.last(), t_bc]
                s8, s4, sx = [P, 8, 64], [P, NCH, P], [P, NCH, 64]
                bc8, bc4 = c8(bc_sum[:, :]), c4(bc_sum[:, :])
                mid = bc8[:, :, 32:33].to_broadcast(s8)
                edge = bc4[:, :, 63:64].to_broadcast(sx)
                end = bc4[:, :, P - 1:P].to_broadcast(s4)
                decayed(c8(q_in[:, :]), c8(q[:, h, :]), bc8, mid, s8, prev + [made[h]])
                t_kin = decayed(c8(k_in[:, :]), c8(k[:, h, :]), mid, bc8, s8, [made[GLA_H + h]])
                decayed(q_x[:, :, :], c4(q[:, h, :])[:, :, 64:P], bc4[:, :, 64:P], edge, sx, [])
                t_x = decayed(k_x[:, :, :], c4(k[:, h, :])[:, :, 0:64], edge, bc4[:, :, 0:64], sx, [])
                t_kd = decayed(c4(kd[:, h, :]), c4(k[:, h, :]), end, bc4, s4, [])
                t = act.op(lambda e: e.activation(ex[:, :], bc_sum[:, :], ACT.Exp), [t_kd])
                dve.op(lambda e, h=h: e.tensor_tensor(e_q[:, h, :], q[:, h, :], ex[:, :], ALU.mult), [t])
                t_ge = dve.op(lambda e, h=h: e.tensor_copy(g_end[:, h, :], c4(ex[:, :])[:, :, P - 1]), [t])
                b, bank, free = work_banks.take()
                b4 = bank[:, :].rearrange("p (c i) -> p c i", c=NCH)
                for c in range(NCH):
                    o = c * P
                    mm(b4[0:64, c, 0:64], k_in[:, o:o + 64], q_in[:, o:o + 64],
                       after=[t_kin, t_x] + list(free), signal=False)
                    mm(b4[0:64, c, 64:P], k_x[:, c, :], q_x[:, c, :], signal=False)
                for c in range(NCH):
                    o = c * P
                    t = mm(b4[64:P, c, 64:P], k_in[:, o + 64:o + P], q_in[:, o + 64:o + P], signal=(c == NCH - 1))
                m4 = const("incl_t")[:, None, :].to_broadcast([P, NCH, P])
                t1 = dve.op(lambda e, b4=b4: e.tensor_tensor(a_t[0:64, :, :], b4[0:64, :, :], m4[0:64, :, :],
                                                             ALU.mult), [t, t_az])
                t_at = dve.op(lambda e, b4=b4: e.tensor_tensor(a_t[64:P, :, 64:P], b4[64:P, :, 64:P],
                                                               m4[64:P, :, 64:P], ALU.mult), [t1])
                work_banks.give(b, t_at)
                for eh in range(2):
                    b, bank, free = work_banks.take()
                    for c in range(NCH):
                        t = mm(bank[:, c * P:(c + 1) * P], v[:, c, (2 * h + eh) * P:(2 * h + eh + 1) * P],
                               a_t[:, c, :], after=[t_at, t_v] + list(free), signal=(c == NCH - 1))
                    t = act.op(lambda e, bank=bank, n=2 * h + eh: e.activation(o_t[:, n, :], bank[:, :], ACT.Copy),
                               [t])
                    work_banks.give(b, t)
            fence()

        state = sb(st, "gla_state", [P, GLA_H, 2 * P])
        kd_tm = sb(st, "gla_kdtm", [P, GLA_H, P])
        t_state = None
        for c in range(NCH):
            cut = slice(c * P, (c + 1) * P)
            if c > 0:
                for half in range(2):
                    b, bank, free = work_banks.take()
                    for j in range(4):
                        n = 4 * half + j
                        t = mm(bank[:, j * P:(j + 1) * P], state[:, n // 2, (n % 2) * P:(n % 2 + 1) * P],
                               e_q[:, n // 2, cut], after=[t_state] + list(free), signal=(j == 3))
                    t = dve.op(lambda e, bank=bank, half=half, cut=cut: e.tensor_tensor(
                        o_t[:, 4 * half:4 * half + 4, cut], o_t[:, 4 * half:4 * half + 4, cut],
                        bank[:, :].rearrange("p (n i) -> p n i", n=4), ALU.add), [t])
                    work_banks.give(b, t)
            if c < NCH - 1:
                b, bank, free = work_banks.take()
                for h in range(GLA_H):
                    t = transpose(bank[:, h * P:(h + 1) * P], kd[:, h, cut], after=free, signal=(h == GLA_H - 1))
                t_tm = act.op(lambda e, bank=bank: e.activation(kd_tm[:, :, :].rearrange("p h i -> p (h i)"),
                                                               bank[:, :], ACT.Copy), [t])
                work_banks.give(b, t_tm)
                for half in range(2):
                    b, bank, free = work_banks.take()
                    for j in range(2):
                        h = 2 * half + j
                        t = mm(bank[:, j * 256:(j + 1) * 256], kd_tm[:, h, :], v[:, c, h * 256:(h + 1) * 256],
                               after=[t_tm] + list(free), signal=(j == 1))
                    if c == 0:
                        t_state = dve.op(lambda e, bank=bank, half=half: e.tensor_copy(
                            state[:, 2 * half:2 * half + 2, :].rearrange("p h i -> p (h i)"), bank[:, :]), [t])
                    else:
                        for j in range(2):
                            h = 2 * half + j
                            t_state = dve.op(lambda e, bank=bank, h=h, j=j, c=c: e.scalar_tensor_tensor(
                                out=state[:, h, :], in0=state[:, h, :], scalar=g_end[:, h, c:c + 1],
                                in1=bank[:, j * 256:(j + 1) * 256], op0=ALU.mult, op1=ALU.add), [t])
                    work_banks.give(b, t_state)

    def cross_attention():
        with ExitStack() as outer:
            fence()
            mk = sb(outer, "xk", [P, DT, MEM])
            mv = sb(outer, "xv", [P, 2, D])
            with ExitStack() as st:
                mem_t = sb(st, "mem_t", [P, DT, MEM])
                m_hi = sb(st, "m_hi", [P, DT, MEM], F32R)
                m_lo = sb(st, "m_lo", [P, DT, MEM], F32R)
                tm = load(mem_t[:, :, :], dram["mem_t"].rearrange("(k p) t -> p k t", p=P),
                          after=everything())
                act.wait([tm])
                dve.wait([tm])
                m_ready = norm_to_h(st, "mem", lambda k: mem_t[:, k, :], lambda k: param("norm_mem_g", k, k + 1),
                                    None, MEM, m_hi, m_lo)

                def take_k(n, ps, tok):
                    return [act.op(lambda e: e.activation(mk[:, n, :], ps, ACT.Copy), [tok])]

                def take_v(i, m, ps, tok):
                    return [act.op(lambda e: e.activation(mv[:, m, i * PW:(i + 1) * PW], ps, ACT.Copy), [tok])]

                gemm("xk", 0, m_hi, m_lo, MEM, lambda k: m_ready[k], take_k)
                gemm("xv", 0, m_hi, m_lo, MEM, lambda k: m_ready[k], take_v, token_major=True)
                fence()
            with ExitStack() as st:
                h_ready = norm_to_h(st, "xn", lambda k: x_t[:, k, :], lambda k: param("norm_xattn_g", k, k + 1),
                                    None, T, h_hi, h_lo)
                q = sb(st, "xq", [P, DT, T])

                def take_q(n, ps, tok):
                    return [act.op(lambda e: e.activation(q[:, n, :], ps, ACT.Copy), [tok])]

                gemm("xq", 0, h_hi, h_lo, T, lambda k: h_ready[k], take_q)
                t_q = act.last()
                pe.wait([t_q])
                scale = (D // XA_H) ** -0.5
                probs = Ring([sb(st, f"xp{i}", [P, 4, MEM]) for i in range(2)])
                pts = Ring([sb(st, f"xpt{i}", [P, 2, T]) for i in range(2)])
                stat = Ring([sb(st, f"xstat{i}", [P, 12]) for i in range(2)])
                ys = Ring([sb(st, f"xy{i}", [P, T]) for i in range(2)])
                o_rdy = {}
                for h in range(XA_H):
                    ip, p, rdp = probs.take()
                    is_, s, rds = stat.take()
                    for half in range(2):
                        b, bank, free = work_banks.take()
                        for j in range(2):
                            m = 2 * half + j
                            for kk in range(2):
                                t = mm(bank[:, j * MEM:(j + 1) * MEM], q[:, 2 * h + kk, m * P:(m + 1) * P],
                                       mk[:, 2 * h + kk, :], start=(kk == 0), stop=(kk == 1), after=free,
                                       signal=(j == 1 and kk == 1))
                        t = dve.op(lambda e, bank=bank, s=s, half=half: e.tensor_reduce(
                            s[:, 2 * half:2 * half + 2], bank[:, :].rearrange("p (a b) -> p a b", a=2), AX, ALU.max),
                            [t] + list(rds))
                        t = dve.op(lambda e, s=s, half=half: e.tensor_scalar(
                            s[:, 2 * half:2 * half + 2], s[:, 2 * half:2 * half + 2], -scale, None, ALU.mult), [t])
                        for j in range(2):
                            m = 2 * half + j
                            t = act.op(lambda e, bank=bank, s=s, p=p, m=m, j=j: e.activation(
                                p[:, m, :], bank[:, j * MEM:(j + 1) * MEM], ACT.Exp, bias=s[:, m:m + 1], scale=scale,
                                accum_out=s[:, 4 + m:5 + m]), [t] + list(rdp))
                        work_banks.give(b, t)
                    t = dve.op(lambda e, s=s: e.reciprocal(s[:, 8:12], s[:, 4:8]), [t])
                    t_p = dve.op(lambda e, s=s, p=p: e.tensor_tensor(
                        p[:, :, :], p[:, :, :], s[:, 8:12][:, :, None].to_broadcast([P, 4, MEM]), ALU.mult), [t])
                    stat.give(is_, t_p)
                    it, pt, rdt = pts.take()
                    for kt in range(2):
                        b, bank, free = work_banks.take()
                        for m in range(4):
                            t = transpose(bank[:, m * P:(m + 1) * P], p[:, m, kt * P:(kt + 1) * P],
                                          after=[t_p] + list(free), signal=(m == 3))
                        t2 = act.op(lambda e, bank=bank, pt=pt, kt=kt: e.activation(pt[:, kt, :], bank[:, :], ACT.Copy),
                                    [t] + list(rdt))
                        work_banks.give(b, t2)
                    probs.give(ip, t)
                    for eh in range(2):
                        n = 2 * h + eh
                        b, bank, free = work_banks.take()
                        for kt in range(2):
                            t = mm(bank[:, :], mv[:, kt, n * P:(n + 1) * P], pt[:, kt, :], start=(kt == 0),
                                   stop=(kt == 1), after=[t2] + list(free), signal=(kt == 1))
                        iy, y, rdy = ys.take()
                        ty = act.op(lambda e, bank=bank, y=y: e.activation(y[:, :], bank[:, :], ACT.Copy),
                                    [t] + list(rdy))
                        work_banks.give(b, ty)
                        o_rdy[n] = split(h_hi[:, n, :], h_lo[:, n, :], y[:, :], [ty])
                        ys.give(iy, o_rdy[n])
                    pts.give(it, t)
                gemm("xo", 0, h_hi, h_lo, T, lambda k: o_rdy[k], add_to_x)
                fence()

    def mlp():
        with ExitStack() as st:
            h_ready = norm_to_h(st, "mlp", lambda k: x_t[:, k, :], lambda k: param("norm_mlp_g", k, k + 1),
                                None, T, h_hi, h_lo)
            f_hi = sb(st, "mlp_hi", [P, 8, T], F32R)
            f_lo = sb(st, "mlp_lo", [P, 8, T], F32R)
            relu = Ring([sb(st, f"relu{i}", [P, T]) for i in range(2)])
            hidden_free = [None]
            for blk in range(F1 // D):
                f_ready = {}

                def take_hidden(n, ps, tok):
                    i, r, rd = relu.take()
                    a = act.op(lambda e: e.activation(r[:, :], ps, ACT.Relu), [tok] + list(rd))
                    t = dve.op(lambda e: e.tensor_tensor(r[:, :], r[:, :], r[:, :], ALU.mult), [a])
                    f_ready[n] = split(f_hi[:, n, :], f_lo[:, n, :], r[:, :], [t, hidden_free[0]])
                    relu.give(i, f_ready[n])
                    return [a]

                gemm_part("mlp1", 0, blk * 4, blk * 4 + 4, h_hi, h_lo, T, lambda k: h_ready[k], take_hidden)
                gemm("mlp2", blk, f_hi, f_lo, T, lambda k: f_ready[k], add_to_x)
                hidden_free[0] = (pe.sem, pe.count)
            fence()

    def gemm_part(key, block, first, last, *args):
        every = where[key][block]
        where[key][block] = every[first:last]
        gemm(key, block, *args)
        where[key][block] = every

    def modulation():
        with ExitStack() as st:
            fence()
            sil = sb(st, "sil", [P, 16])
            c_in = prm[:, PARAM_AT["c"][0]:PARAM_AT["c"][0] + 16]
            a = act.op(lambda e: e.activation(sil[:, :], c_in, ACT.Tanh, scale=0.5))
            t = dve.op(lambda e: e.scalar_tensor_tensor(out=sil[:, :], in0=sil[:, :], scalar=1.0, in1=c_in,
                                                        op0=ALU.add, op1=ALU.mult), [a])
            t_sil = dve.op(lambda e: e.tensor_scalar(sil[:, :], sil[:, :], 0.5, None, ALU.mult), [t])
            AW = 1024
            wbuf = [sb(st, f"ada_w{i}", [P, 2, AW]) for i in range(3)]
            ring_sems = [top.enter_context(nc.semaphore(f"ada_loaded{i}")) for i in range(3)]
            accs = Ring([sb(st, f"ada_acc{i}", [P, AW]) for i in range(2)])
            acc_c = sb(st, "ada_accc", [P, AW])
            sp.wait(everything())
            w_free = [None] * 3
            n = 0
            for layer in range(2):
                for j in range(6):
                    i, acc, rd = accs.take()
                    ctx_too = layer == 0 and j < 2
                    for kp in range(DT // 2):
                        slot = n % 3
                        sp.wait([w_free[slot]])
                        src = dram[f"ada_w{layer}"][j, kp]
                        sp.items.append(lambda e, slot=slot, src=src: e.dma_start(
                            wbuf[slot][:, :, :], src).then_inc(ring_sems[slot], 16))
                        landed = (ring_sems[slot], 16 * (n // 3 + 1))
                        for kk in range(2):
                            k = 2 * kp + kk
                            for which, dst in ((0, acc), (1, acc_c)) if ctx_too else ((0, acc),):
                                w = wbuf[slot][:, kk, :]
                                col = sil[:, 8 * which + k:8 * which + k + 1]
                                after = [landed, t_sil, dve.last()] + (list(rd) if k == 0 else []) + \
                                    ([pe.last()] if which and k == 0 else [])
                                if k == 0:
                                    t = dve.op(lambda e, dst=dst, w=w, col=col: e.tensor_scalar(
                                        dst[:, :], w, col, None, ALU.mult), after)
                                else:
                                    t = dve.op(lambda e, dst=dst, w=w, col=col: e.scalar_tensor_tensor(
                                        out=dst[:, :], in0=w, scalar=col, in1=dst[:, :], op0=ALU.mult, op1=ALU.add),
                                        after)
                        w_free[slot] = t
                        n += 1
                    for which, src_acc in ((0, acc), (1, acc_c)) if ctx_too else ((0, acc),):
                        b, bank, free = work_banks.take()
                        for c in range(8):
                            tok = mm(bank[:, c:c + 1], src_acc[:, c * P:(c + 1) * P], const("ones")[:, 0:1],
                                     after=[t] + list(free), signal=(c == 7))
                        at = 96 + 8 * j if which else 48 * layer + 8 * j
                        bias = param(f"ada_b{layer}", 8 * j, 8 * j + 8)
                        td = dve.op(lambda e, bank=bank, at=at, bias=bias: e.tensor_tensor(
                            mod[:, at:at + 8], bank[:, 0:8], bias, ALU.add), [tok])
                        work_banks.give(b, td)
                    accs.give(i, tok)
            for at, gain in ((8, "norm1_g0"), (32, "norm2_g0"), (56, "norm1_g1"), (80, "norm2_g1"), (104, "norm1_g0")):
                td = dve.op(lambda e, at=at, gain=gain: e.scalar_tensor_tensor(
                    out=mod[:, at:at + 8], in0=mod[:, at:at + 8], scalar=1.0, in1=param(gain),
                    op0=ALU.add, op1=ALU.mult), [td])
            lm = prm[0:64, PARAM_AT["lam"][0]:PARAM_AT["lam"][0] + 4].rearrange("p (a b) -> p a b", b=2)
            pr = sb(st, "lam_pr", [64, 2])
            t = dve.op(lambda e: e.tensor_tensor(pr[:, :], lm[:, :, 0], lm[:, :, 1], ALU.mult))
            b, bank, free = work_banks.take()
            t = mm(bank[:, 0:2], const("ones")[0:64, :], pr[:, :], after=[t] + list(free))
            a = act.op(lambda e, bank=bank: e.activation(lam_col[:, 0:2], bank[:, 0:2], ACT.Exp), [t])
            work_banks.give(b, a)
            t = dve.op(lambda e: e.tensor_tensor(lam_col[:, 2:3], lam_col[:, 1:2], lam_col[:, 0:1], ALU.subtract), [a])
            dve.op(lambda e: e.tensor_scalar(lam_col[:, 3:4], lam_col[:, 2:3], -LAM_INIT, None, ALU.add), [t])
            fence()

    def add_gated(layer, j):
        def take(n, ps, tok):
            g = mod[:, 48 * layer + 8 * j + n:48 * layer + 8 * j + n + 1]
            return [dve.op(lambda e: e.scalar_tensor_tensor(out=x_t[:, n, :], in0=ps, scalar=g, in1=x_t[:, n, :],
                                                            op0=ALU.mult, op1=ALU.add), [tok])]
        return take

    def mod_col(at):
        return lambda k: mod[:, at + k:at + k + 1]

    def swiglu(layer):
        with ExitStack() as st:
            base = 48 * layer
            h_ready = norm_to_h(st, f"ffn{layer}", lambda k: x_t[:, k, :], mod_col(base + 32), mod_col(base + 24),
                                T, h_hi, h_lo)
            f_hi = sb(st, f"ffn_hi{layer}", [P, 8, T], F32R)
            f_lo = sb(st, f"ffn_lo{layer}", [P, 8, T], F32R)
            tmp = Ring([sb(st, f"ffn_t{layer}{i}", [P, T]) for i in range(2)])
            hidden_free = [None]
            for blk, (k0, nk) in enumerate(k_blocks(F2)):
                f_ready, held = {}, {}

                def take_hidden(n, ps, tok):
                    f, part = n // 2, n % 2
                    if part == 0:
                        i, y, rd = tmp.take()
                        a = act.op(lambda e: e.activation(y[:, :], ps, ACT.Tanh, scale=0.5), [tok] + list(rd))
                        t = dve.op(lambda e: e.scalar_tensor_tensor(out=y[:, :], in0=y[:, :], scalar=1.0, in1=ps,
                                                                    op0=ALU.add, op1=ALU.mult), [a])
                        held[f] = (i, y, t)
                        return [t]
                    i, y, t = held.pop(f)
                    t = dve.op(lambda e: e.scalar_tensor_tensor(out=y[:, :], in0=y[:, :], scalar=0.5, in1=ps,
                                                                op0=ALU.mult, op1=ALU.mult), [t, tok])
                    f_ready[f] = split(f_hi[:, f, :], f_lo[:, f, :], y[:, :], [t, hidden_free[0]])
                    tmp.give(i, f_ready[f])
                    return [t]

                gemm_part(f"ffn1_{layer}", 0, k0, k0 + nk, h_hi, h_lo, T, lambda k: h_ready[k], take_hidden)
                gemm(f"ffn2_{layer}", blk, f_hi, f_lo, T, lambda k: f_ready[k], add_gated(layer, 5))
                hidden_free[0] = (pe.sem, pe.count)
            fence()

    def diff_attention():
        NK = CTX + T
        KT = NK // P
        with ExitStack() as outer:
            k_all = sb(outer, "da_k", [P, DA_H, NK])
            v_all = sb(outer, "da_v", [P, KT, D])
            q = sb(outer, "da_q", [P, DA_H, T])
            with ExitStack() as st:
                c_hi = sb(st, "c_hi", [P, DT, CTX], F32R)
                c_lo = sb(st, "c_lo", [P, DT, CTX], F32R)
                with ExitStack() as s2:
                    ctx_t = sb(s2, "ctx_t", [P, DT, CTX])
                    fence()
                    tc = load(ctx_t[:, :, :], dram["ctx_t"].rearrange("(k p) t -> p k t", p=P),
                              after=everything())
                    act.wait([tc])
                    dve.wait([tc])
                    c_ready = norm_to_h(s2, "ctx", lambda k: ctx_t[:, k, :], mod_col(104), mod_col(96), CTX, c_hi, c_lo)
                    fence()
                with ExitStack() as s2:
                    h_ready = norm_to_h(s2, "da", lambda k: x_t[:, k, :], mod_col(8), mod_col(0), T, h_hi, h_lo)
                    fence()
                with ExitStack() as s2:
                    cosb = sb(s2, "rope_cos", [P, T])
                    sinb = sb(s2, "rope_sin", [P, T])
                    fence()
                    tr = [load(cosb[:, :], dram["rope_cos"], after=everything()),
                          load(sinb[:, :], dram["rope_sin"], after=everything())]
                    rr = Ring([sb(s2, f"rope_t{i}", [P, 2, T]) for i in range(1)])

                    def rope_into(dst):
                        def take(n, ps, tok):
                            i, buf, rd = rr.take()
                            a = act.op(lambda e: e.activation(buf[:, 0, :], ps, ACT.Copy), [tok] + list(rd))
                            swap = [(p + 16) % 32 for p in range(32)]
                            t = dve.op(lambda e: e.stream_shuffle(buf[:, 1, :], buf[:, 0, :], swap), [a])
                            t1 = pool.op(lambda e: e.tensor_tensor(buf[:, 0, :], buf[:, 0, :], cosb[:, :], ALU.mult),
                                         [t] + tr)
                            t2 = dve.op(lambda e: e.tensor_tensor(buf[:, 1, :], buf[:, 1, :], sinb[:, :], ALU.mult),
                                        [t] + tr)
                            t = dve.op(lambda e: e.tensor_tensor(dst(n), buf[:, 0, :], buf[:, 1, :], ALU.add), [t1, t2])
                            rr.give(i, t)
                            return [a]
                        return take

                    for i in range(len(where["da_k"][0])):
                        hi, lo, nk, width = panel("da_k", 0, i)
                        for c in range(width // P):
                            n = 2 * i + c
                            cut = slice(c * P, (c + 1) * P)
                            w = [(hi[:, k, cut], lo[:, k, cut]) for k in range(nk)]
                            b, bank, free = gemm_banks.take()
                            tok = products(bank[:, 0:CTX], [(w[k], (c_hi[:, k, :], c_lo[:, k, :])) for k in range(nk)],
                                           after=list(free) + [c_ready[k] for k in range(nk)])
                            gemm_banks.give(b, act.op(lambda e, n=n, bank=bank: e.activation(
                                k_all[:, n, 0:CTX], bank[:, 0:CTX], ACT.Copy), [tok]))
                            b, bank, free = gemm_banks.take()
                            tok = products(bank[:, :], [(w[k], (h_hi[:, k, :], h_lo[:, k, :])) for k in range(nk)],
                                           after=list(free) + [h_ready[k] for k in range(nk)])
                            if c == width // P - 1:
                                tok = end_panel()
                            gemm_banks.give(b, *rope_into(lambda n: k_all[:, n, CTX:NK])(n, bank[:, :], tok))
                    for i in range(len(where["da_v"][0])):
                        hi, lo, nk, width = panel("da_v", 0, i)
                        for m in range(KT):
                            a_hi, a_lo, at = (c_hi, c_lo, m) if m < CTX // P else (h_hi, h_lo, m - CTX // P)
                            cut = slice(at * P, (at + 1) * P)
                            b, bank, free = gemm_banks.take()
                            tok = products(bank[:, 0:width], [((a_hi[:, k, cut], a_lo[:, k, cut]),
                                                               (hi[:, k, :], lo[:, k, :])) for k in range(nk)],
                                           after=free)
                            if m == KT - 1:
                                tok = end_panel()
                            gemm_banks.give(b, act.op(lambda e, m=m, i=i, bank=bank: e.activation(
                                v_all[:, m, i * PW:(i + 1) * PW], bank[:, 0:PW], ACT.Copy), [tok]))
                    gemm("da_q", 0, h_hi, h_lo, T, lambda k: h_ready[k], rope_into(lambda n: q[:, n, :]))
                    fence()
            attend(outer, q, k_all, v_all, NK, KT)
            gemm("da_o", 0, h_hi, h_lo, T, lambda k: None, add_gated(0, 2))
            fence()

    def attend(s2, q, k_all, v_all, NK, KT):
        scale = 64 ** -0.5
        pm = Ring([sb(s2, f"da_p{i}", [P, 2, NK]) for i in range(1)])
        pts = Ring([sb(s2, f"da_pt{i}", [P, KT, T]) for i in range(1)])
        stat = Ring([sb(s2, f"da_stat{i}", [P, 12]) for i in range(2)])
        y = sb(s2, "da_y", [P, T])
        sq = sb(s2, "da_sq", [P, T])
        t_y = None
        for h in range(DA_H):
            it, pt, rdt = pts.take()
            for m in range(T // P):
                ip, p, rdp = pm.take()
                is_, s, rds = stat.take()
                for mp in range(2):
                    rows = slice(64 * mp, 64 * mp + 64)
                    b1, bk1, free1 = work_banks.take()
                    b2, bk2, free2 = work_banks.take()
                    mm(bk1[:, :], q[rows, h, m * P:(m + 1) * P], k_all[rows, h, 0:512],
                       after=list(free1) + list(free2), signal=False)
                    t = mm(bk2[:, 0:256], q[rows, h, m * P:(m + 1) * P], k_all[rows, h, 512:768])
                    c = 6 * mp
                    ta = dve.op(lambda e, bk1=bk1, s=s, c=c: e.tensor_reduce(s[:, c:c + 1], bk1[:, :], AX, ALU.max),
                                [t] + list(rds))
                    tb = dve.op(lambda e, bk2=bk2, s=s, c=c: e.tensor_reduce(s[:, c + 1:c + 2], bk2[:, 0:256], AX,
                                                                             ALU.max), [t])
                    t = dve.op(lambda e, s=s, c=c: e.tensor_tensor(s[:, c:c + 1], s[:, c:c + 1], s[:, c + 1:c + 2],
                                                                   ALU.max), [ta, tb])
                    t = dve.op(lambda e, s=s, c=c: e.tensor_scalar(s[:, c + 1:c + 2], s[:, c:c + 1], -scale, None,
                                                                   ALU.mult), [t])
                    a1 = act.op(lambda e, bk1=bk1, s=s, c=c, p=p, mp=mp: e.activation(
                        p[:, mp, 0:512], bk1[:, :], ACT.Exp, bias=s[:, c + 1:c + 2], scale=scale,
                        accum_out=s[:, c + 2:c + 3]), [t] + list(rdp))
                    a2 = act.op(lambda e, bk2=bk2, s=s, c=c, p=p, mp=mp: e.activation(
                        p[:, mp, 512:768], bk2[:, 0:256], ACT.Exp, bias=s[:, c + 1:c + 2], scale=scale,
                        accum_out=s[:, c + 3:c + 4]))
                    work_banks.give(b1, a1)
                    work_banks.give(b2, a2)
                    t = dve.op(lambda e, s=s, c=c: e.tensor_tensor(s[:, c + 4:c + 5], s[:, c + 2:c + 3],
                                                                   s[:, c + 3:c + 4], ALU.add), [a1, a2])
                    t = dve.op(lambda e, s=s, c=c: e.reciprocal(s[:, c + 5:c + 6], s[:, c + 4:c + 5]), [t])
                t = dve.op(lambda e, s=s: e.tensor_tensor(s[:, 11:12], s[:, 11:12], lam_col[:, 3:4], ALU.mult), [t])
                t = dve.op(lambda e, s=s, p=p: e.tensor_scalar(p[:, 0, :], p[:, 0, :], s[:, 5:6], None, ALU.mult), [t])
                t_p = dve.op(lambda e, s=s, p=p: e.scalar_tensor_tensor(
                    out=p[:, 0, :], in0=p[:, 1, :], scalar=s[:, 11:12], in1=p[:, 0, :], op0=ALU.mult, op1=ALU.add), [t])
                stat.give(is_, t_p)
                for half in range(2):
                    b, bank, free = work_banks.take()
                    for j in range(3):
                        kt = 3 * half + j
                        t = transpose(bank[:, j * P:(j + 1) * P], p[:, 0, kt * P:(kt + 1) * P],
                                      after=[t_p] + list(free), signal=(j == 2))
                    t2 = act.op(lambda e, bank=bank, pt=pt, half=half, m=m: e.activation(
                        pt[:, 3 * half:3 * half + 3, m * P:(m + 1) * P],
                        bank[:, 0:3 * P].rearrange("p (a b) -> p a b", a=3), ACT.Copy), [t] + list(rdt))
                    work_banks.give(b, t2)
                pm.give(ip, t)
            b, bank, free = work_banks.take()
            for kt in range(KT):
                t = mm(bank[:, :], v_all[:, kt, h * P:(h + 1) * P], pt[:, kt, :], start=(kt == 0),
                       stop=(kt == KT - 1), after=[t2] + list(free), signal=(kt == KT - 1))
            pts.give(it, t)
            ty = act.op(lambda e, bank=bank: e.activation(y[:, :], bank[:, :], ACT.Copy), [t, t_y])
            ts = act.op(lambda e, bank=bank: e.activation(sq[:, :], bank[:, :], ACT.Square))
            work_banks.give(b, ts)
            b, bank, free = work_banks.take()
            t = mm(bank[:, :], const("ones"), sq[:, :], after=[ts] + list(free))
            t = act.op(lambda e, bank=bank: e.activation(sq[:, :], bank[:, :], ACT.Sqrt, bias=param("eps"),
                                                         scale=1.0 / P), [t])
            work_banks.give(b, t)
            t = dve.op(lambda e: e.reciprocal(sq[:, :], sq[:, :]), [t, ty])
            t = dve.op(lambda e: e.scalar_tensor_tensor(out=y[:, :], in0=y[:, :], scalar=param("subln_g"),
                                                        in1=sq[:, :], op0=ALU.mult, op1=ALU.mult), [t])
            t = dve.op(lambda e: e.tensor_scalar(y[:, :], y[:, :], 1.0 - LAM_INIT, None, ALU.mult), [t])
            t_y = split(h_hi[:, h, :], h_lo[:, h, :], y[:, :], [t])
        fence()

    def short_conv():
        with ExitStack() as st:
            h_ready = norm_to_h(st, "sc", lambda k: x_t[:, k, :], mod_col(56), mod_col(48), T, h_hi, h_lo)
            conv = sb(st, "sc_conv", [P, DT, T])
            f_hi = sb(st, "sc_hi", [P, 8, T], F32R)
            f_lo = sb(st, "sc_lo", [P, 8, T], F32R)
            zs = [sb(st, f"sc_z{i}", [P, T + 2]) for i in range(2)]
            fence()
            pads = []
            for z in zs:
                pool.op(lambda e, z=z: e.memset(z[:, 0:1], 0.0))
                pads.append(pool.op(lambda e, z=z: e.memset(z[:, T + 1:T + 2], 0.0)))
            ring = Ring(zs)
            ring.free = [(p,) for p in pads]
            held, made = {}, {}

            def take_cu(n, ps, tok):
                f, part = n // 2, n % 2
                if part == 0:
                    i, z, rd = ring.take()
                    a = act.op(lambda e: e.activation(z[:, 1:T + 1], ps, ACT.Copy), [tok] + list(rd))
                    held[f] = (i, z, a)
                    return [a]
                i, z, a = held.pop(f)
                t0 = dve.op(lambda e: e.tensor_tensor(z[:, 1:T + 1], z[:, 1:T + 1], ps, ALU.mult), [a, tok])
                w = lambda j: param("sc_conv_w", 3 * f + j, 3 * f + j + 1)
                t = dve.op(lambda e: e.tensor_scalar(conv[:, f, :], z[:, 0:T], w(0), None, ALU.mult), [t0])
                for j in range(1, 3):
                    t = dve.op(lambda e, j=j: e.scalar_tensor_tensor(
                        out=conv[:, f, :], in0=z[:, j:j + T], scalar=w(j), in1=conv[:, f, :],
                        op0=ALU.mult, op1=ALU.add), [t])
                ring.give(i, t)
                made[f] = t
                return [t0]

            gemm("sc_cu", 0, h_hi, h_lo, T, lambda k: h_ready[k], take_cu)
            f_ready = {}

            def take_b(n, ps, tok):
                t = dve.op(lambda e: e.tensor_tensor(conv[:, n, :], conv[:, n, :], ps, ALU.mult), [tok, made[n]])
                f_ready[n] = split(f_hi[:, n, :], f_lo[:, n, :], conv[:, n, :], [t])
                return [t]

            gemm("sc_b", 0, h_hi, h_lo, T, lambda k: h_ready[k], take_b)
            gemm("sc_o", 0, f_hi, f_lo, T, lambda k: f_ready[k], add_gated(1, 2))
            fence()

    def finish_block_one():
        with ExitStack() as st:
            fence()
            r = rms_stats(st, "b1", lambda k: x_t[:, k, :], DT, T, D)
            for k in range(DT):
                dve.op(lambda e, k=k: e.scalar_tensor_tensor(
                    out=x_t[:, k, :], in0=x_t[:, k, :], scalar=param("norm_final_g", k, k + 1), in1=rstd[:, :],
                    op0=ALU.mult, op1=ALU.mult), [r])
            fence()

    def final():
        with ExitStack() as st:
            fence()
            r = rms_stats(st, "fin", lambda k: x_t[:, k, :], DT, T, D)
            out_v = out_t.rearrange("(k p) t -> p k t", p=P)
            stored = top.enter_context(nc.semaphore("stored"))
            for k in range(DT):
                t = dve.op(lambda e, k=k: e.scalar_tensor_tensor(
                    out=x_t[:, k, :], in0=x_t[:, k, :], scalar=param("final_g", k, k + 1), in1=rstd[:, :],
                    op0=ALU.mult, op1=ALU.mult), [r])
                sp.wait([t])
                sp.items.append(lambda e, k=k: e.dma_start(out_v[:, k, :], x_t[:, k, :]).then_inc(stored, 16))
            sp.items.append(lambda e: e.wait_ge(stored, 16 * DT))

    mixer()
    cross_attention()
    mlp()
    finish_block_one()
    modulation()
    diff_attention()
    swiglu(0)
    short_conv()
    swiglu(1)
    final()
    for q in engines + (sp,):
        q.flush()
    top.close()


def lay_params(inputs):
    f = lambda name: np.asarray(inputs[name])
    cols = lambda a: a.reshape(-1, P).T
    spread = lambda a: np.broadcast_to(a.reshape(1, -1), (P, a.size))
    lam = np.zeros((P, 4), np.float32)
    lam[0:64, :] = f("da_lambda_2")[0].T
    conv = f("gdn_conv_w")[0].reshape(4, 24, P).transpose(2, 1, 0).reshape(P, 96)
    sc = f("sc_conv_w_2")[0].reshape(3, 8, P).transpose(2, 1, 0).reshape(P, 24)
    table = {
        "norm_mix_g": cols(f("norm_mix_g")), "gdn_conv_w": conv, "a_log": spread(f("gdn_a_log")),
        "dt_bias": spread(f("gdn_dt_bias")), "gdn_norm_g": cols(f("gdn_norm_g")),
        "gla_b_gate": cols(f("gla_b_gate")), "gla_norm_g": cols(f("gla_norm_g")),
        "norm_xattn_g": cols(f("norm_xattn_g")), "norm_mem_g": cols(f("norm_mem_g")),
        "norm_mlp_g": cols(f("norm_mlp_g")), "norm_final_g": cols(f("norm_final_g")),
        "c": cols(f("c_2")), "c_ctx": cols(f("c_ctx_2")),
        "ada_b0": cols(f("ada_b_2")[0]), "ada_b1": cols(f("ada_b_2")[1]),
        "norm1_g0": cols(f("norm1_g_2")[0]), "norm1_g1": cols(f("norm1_g_2")[1]),
        "norm2_g0": cols(f("norm2_g_2")[0]), "norm2_g1": cols(f("norm2_g_2")[1]),
        "final_g": cols(f("final_g_2")), "lam": lam, "subln_g": cols(f("da_subln_g_2")), "sc_conv_w": sc,
        "eps": np.full((P, 1), EPS, np.float32), "eps4": np.full((P, 1), 4 * EPS, np.float32),
    }
    return np.concatenate([table[name] for name, _ in PARAM_WIDTHS], axis=1)


def shape_constants():
    i = np.arange(P)[:, None]
    j = np.arange(P)[None, :]

    def level(s, row, col):
        return (row // (2 * s) == col // (2 * s)) & (row % (2 * s) >= s) & (col % (2 * s) < s)

    made = {"ident": i == j, "ones": np.ones((P, P)), "incl_t": i <= j, "strict": i > j, "strict_t": i < j,
            "lvl1": level(1, i, j), "lvl1_t": level(1, j, i)}
    for s in (2, 4, 8, 16, 32, 64):
        made[f"lvl{s}_t"] = level(s, j, i)
    return np.concatenate([made[n].astype(np.float32) for n in CONSTS], axis=1)


def rope_constants():
    n = np.arange(T)
    inv = 1.0 / (10000.0 ** (np.arange(0, 32, 2, dtype=np.float32) / np.float32(32)))
    inv = inv.astype(np.float32)
    row, col = (n // 64).astype(np.float32), (n % 64).astype(np.float32)
    ang = np.concatenate([row[None, :] * inv[:, None], col[None, :] * inv[:, None]], 0).astype(np.float32)
    d = np.arange(P) % 64
    which = (d // 32) * 16 + d % 16
    sign = np.where(d % 32 < 16, -1.0, 1.0).astype(np.float32)
    return np.cos(ang)[which].astype(np.float32), (np.sin(ang)[which] * sign[:, None]).astype(np.float32)


def pack(weight, blocks, columns):
    parts = []
    for k0, nk in blocks:
        for cols in columns:
            w = weight[k0 * P:(k0 + nk) * P, cols]
            parts.append(w.reshape(nk, P, len(cols)).transpose(1, 0, 2).reshape(-1))
    return np.concatenate(parts)


def kernel(**inputs):
    import concourse.bacc as bacc
    from concourse.bass_utils import run_bass_kernel_spmd

    f = lambda name: np.asarray(inputs[name])
    cos, sin = rope_constants()
    arrays = {
        "x_t": np.ascontiguousarray(f("x")[0].T), "mem_t": np.ascontiguousarray(f("mem")[0].T),
        "ctx_t": np.ascontiguousarray(f("ctx_2")[0].T), "params": lay_params(inputs),
        "consts": shape_constants(), "rope_cos": cos, "rope_sin": sin,
        "gla_w2": np.ascontiguousarray(f("gla_w_gate2")[0]),
    }
    for layer in range(2):
        a = f("ada_w_2")[layer].reshape(4, 2, P, 6, D).transpose(3, 0, 2, 1, 4)
        arrays[f"ada_w{layer}"] = np.ascontiguousarray(a)
    for key, weight, blocks, columns in panel_plan():
        name, _, layer = weight.partition(".")
        arrays["pack_" + key] = pack(f(name)[int(layer or 0)], blocks, columns)

    nc = bacc.Bacc("TRN2", target_bir_lowering=False, num_devices=1)
    dram = {n: nc.dram_tensor("in_" + n, a.shape, F32, kind="ExternalInput").ap() for n, a in arrays.items()}
    out = nc.dram_tensor("out_t", (D, T), F32, kind="ExternalOutput").ap()
    build_program(nc, dram, out)
    result = run_bass_kernel_spmd(nc, [{"in_" + n: a for n, a in arrays.items()}], core_ids=[0])
    return np.ascontiguousarray(result.results[0]["out_t"].T)[None]
```

```python
from contextlib import ExitStack

import numpy as np
import concourse.bass as bass
from concourse import mybir

F32 = mybir.dt.float32
F32R = mybir.dt.float32r
ACT = mybir.ActivationFunctionType
ALU = mybir.AluOpType
AX = mybir.AxisListType.X

P = 128
D = 1024
DT = D // P
T = 512
MEM = 256
CTX = 256
CHUNK = 128
NCH = T // CHUNK
GDN_H = 8
GLA_H = 4
XA_H = 4
DA_H = 8
F1 = 4096
F2 = 2816
PW = 256
EPS = 1e-6
GLA_TAU = 16.0
LAM_INIT = 0.8 - 0.6 * float(np.exp(-0.3 * 0))

GZ0, GA0, LQ0, LV0, LR0, LG0, GTA0, GTB0 = 3072, 4096, 4112, 5136, 6160, 7184, 7200, 8224

PARAM_WIDTHS = (
    ("norm_mix_g", 8), ("gdn_conv_w", 96), ("a_log", 8), ("dt_bias", 8), ("gdn_norm_g", 1),
    ("gla_b_gate", 4), ("gla_norm_g", 2), ("norm_xattn_g", 8), ("norm_mem_g", 8), ("norm_mlp_g", 8),
    ("norm_final_g", 8),
    ("c", 8), ("c_ctx", 8), ("ada_b0", 48), ("ada_b1", 48), ("norm1_g0", 8), ("norm1_g1", 8),
    ("norm2_g0", 8), ("norm2_g1", 8), ("final_g", 8), ("lam", 4), ("subln_g", 1), ("sc_conv_w", 24),
    ("eps", 1), ("eps4", 1),
)
PARAM_AT = {}
_at = 0
for _name, _width in PARAM_WIDTHS:
    PARAM_AT[_name] = (_at, _width)
    _at += _width
N_PARAMS = _at

N_KEPT = 3
CONSTS = ("ident", "ones", "incl_t", "strict", "strict_t", "lvl1", "lvl1_t",
          "lvl2_t", "lvl4_t", "lvl8_t", "lvl16_t", "lvl32_t", "lvl64_t")


def pair_columns(first, second, n):
    return [list(range(first + i * P, first + (i + 1) * P)) + list(range(second + i * P, second + (i + 1) * P))
            for i in range(n)]


def run_columns(start, n, width=PW):
    return [list(range(start + i * width, start + (i + 1) * width)) for i in range(n // width)]


def k_blocks(k):
    return [(t, min(8, k // P - t)) for t in range(0, k // P, 8)]


def panel_plan():
    full = [(0, 8)]
    plan = [
        ("gates", "w_in", full, [list(range(GA0, GA0 + 16)) + list(range(LG0, LG0 + 16))]),
        ("gdn_qkv", "w_in", full, run_columns(0, 3072)),
        ("gdn_z", "w_in", full, run_columns(GZ0, 1024)),
        ("gate_a", "w_in", full, run_columns(GTA0, 1024)),
        ("branch_a", "w_branch_gdn", full, run_columns(0, D)),
        ("gla_qk", "w_in", full, run_columns(LQ0, 1024)),
        ("gla_v", "w_in", full, run_columns(LV0, 1024)),
        ("gla_r", "w_in", full, run_columns(LR0, 1024)),
        ("gate_b", "w_in", full, run_columns(GTB0, 1024)),
        ("branch_b", "w_branch_gla", full, run_columns(0, D)),
        ("w_out", "w_out", full, run_columns(0, D)),
        ("xk", "xattn_wk", full, run_columns(0, D)),
        ("xv", "xattn_wv", full, run_columns(0, D)),
        ("xq", "xattn_wq", full, run_columns(0, D)),
        ("xo", "xattn_wo", full, run_columns(0, D)),
        ("mlp1", "mlp_w1", full, run_columns(0, F1)),
        ("mlp2", "mlp_w2", k_blocks(F1), run_columns(0, D)),
        ("da_k", "da_wqkv_2", full, run_columns(D, D)),
        ("da_v", "da_wqkv_2", full, run_columns(2 * D, D)),
        ("da_q", "da_wqkv_2", full, run_columns(0, D)),
        ("da_o", "da_wo_2", full, run_columns(0, D)),
        ("ffn1_0", "ffn_w_in_2.0", full, pair_columns(0, F2, F2 // P)),
        ("ffn2_0", "ffn_w_out_2.0", k_blocks(F2), run_columns(0, D)),
        ("sc_cu", "sc_w_in_2", full, pair_columns(D, 2 * D, DT)),
        ("sc_b", "sc_w_in_2", full, run_columns(0, D)),
        ("sc_o", "sc_w_out_2", full, run_columns(0, D)),
        ("ffn1_1", "ffn_w_in_2.1", full, pair_columns(0, F2, F2 // P)),
        ("ffn2_1", "ffn_w_out_2.1", k_blocks(F2), run_columns(0, D)),
    ]
    return plan


def build_program(nc, dram, out_t):
    top = ExitStack()

    class Queue:

        def __init__(self, engine, name):
            self.engine, self.items, self.count = engine, [], 0
            self.sem = top.enter_context(nc.semaphore(name))
            self.seen, self.unsignalled = {}, False

        def wait(self, tokens):
            for token in tokens:
                if token is None:
                    continue
                sem, value = token
                if self.seen.get(sem.name, 0) >= value:
                    continue
                self.seen[sem.name] = value
                self.items.append(lambda e, s=sem, v=value: e.wait_ge(s, v))

        def op(self, issue, after=(), signal=True):
            self.wait(after)
            if not signal:
                self.items.append(issue)
                self.unsignalled = True
                return None
            self.count += 1
            self.unsignalled = False
            self.items.append(lambda e: issue(e).then_inc(self.sem, 1))
            return (self.sem, self.count)

        def last(self):
            return (self.sem, self.count) if self.count else None

        def place(self):
            spot = []
            self.items.append(spot)
            return spot

        def flush(self):
            def run(items):
                for item in items:
                    if isinstance(item, list):
                        run(item)
                    else:
                        item(self.engine)
            run(self.items)

    pe, act, dve, pool, sp = (Queue(e, n) for e, n in (
        (nc.tensor, "pe_done"), (nc.scalar, "act_done"), (nc.vector, "dve_done"),
        (nc.gpsimd, "pool_done"), (nc.sync, "sp_done")))
    engines = (pe, act, dve, pool)

    def everything():
        return [q.last() for q in engines]

    def fence():
        assert not any(q.unsignalled for q in engines)
        marks = everything()
        for q in engines:
            q.wait(marks)

    loads = [0]

    def load(dst, src, after=(), queue=None):
        queue = queue or pool
        sem = top.enter_context(nc.semaphore(f"load{loads[0]}"))
        loads[0] += 1
        queue.wait(after)
        queue.items.append(lambda e: e.dma_start(dst, src).then_inc(sem, 16))
        return (sem, 16)

    def sb(stack, name, shape, dt=F32):
        return stack.enter_context(nc.sbuf_tensor(name, shape, dt))

    x_t = sb(top, "x_t", [P, DT, T])
    h_hi = sb(top, "h_hi", [P, DT, T], F32R)
    h_lo = sb(top, "h_lo", [P, DT, T], F32R)
    N_RAW, N_SPLIT = 2, 2
    w_raw = [sb(top, f"w_raw{i}", [P, DT * PW]) for i in range(N_RAW)]
    w_hi = [sb(top, f"w_hi{i}", [P, DT * PW], F32R) for i in range(N_SPLIT)]
    w_lo = [sb(top, f"w_lo{i}", [P, DT * PW], F32R) for i in range(N_SPLIT)]
    prm = sb(top, "prm", [P, N_PARAMS])
    kept_consts = sb(top, "kept_consts", [P, N_KEPT, P])
    scan_consts = []
    mod = sb(top, "mod", [P, 112])
    rstd = sb(top, "rstd", [P, T])
    lam_col = sb(top, "lam_col", [P, 4])
    tmp_tiles = [sb(top, f"tmp{i}", [P, T]) for i in range(4)]
    banks = [top.enter_context(nc.psum_tensor(f"bank{i}", [P, 512], F32)) for i in range(8)]

    def param(name, a=0, b=None):
        at, width = PARAM_AT[name]
        return prm[:, at + a:at + (width if b is None else b)]

    def const(name):
        i = CONSTS.index(name)
        return kept_consts[:, i, :] if i < N_KEPT else scan_consts[0][:, i - N_KEPT, :]

    class Ring:

        def __init__(self, buffers):
            self.buffers, self.free, self.n = buffers, [()] * len(buffers), 0

        def take(self):
            i = self.n % len(self.buffers)
            self.n += 1
            free, self.free[i] = self.free[i], None
            assert free is not None, "taken before it was given back"
            return i, self.buffers[i], free

        def give(self, i, *readers):
            self.free[i] = readers

    gemm_banks = Ring(banks[0:4])
    work_banks = Ring(banks[4:7])
    tmps = Ring(tmp_tiles)

    raw_loaded = [top.enter_context(nc.semaphore(f"raw_loaded{i}")) for i in range(N_RAW)]
    hi_made = top.enter_context(nc.semaphore("hi_made"))
    lo_made = top.enter_context(nc.semaphore("lo_made"))

    plan, offset, where = panel_plan(), {}, {}
    for key, weight, blocks, columns in plan:
        where[key] = []
        offset.setdefault(key, 0)
        at = 0
        for k0, nk in blocks:
            row = []
            for cols in columns:
                row.append((at, nk, len(cols)))
                at += P * nk * len(cols)
            where[key].append(row)
    panel_n = [0]
    panel_end = []
    spots = {}

    def leave_spot():
        n = panel_n[0]
        spots[n] = (sp.place(), act.place(), dve.place())

    def panel(key, block, i):
        n = panel_n[0]
        at, nk, width = where[key][block][i]
        size = nk * width
        raw, raw_sem, raw_n = w_raw[n % N_RAW], raw_loaded[n % N_RAW], n // N_RAW + 1
        hi, lo = w_hi[n % N_SPLIT], w_lo[n % N_SPLIT]
        sp_spot, act_spot, dve_spot = spots.pop(n)
        if n >= N_RAW:
            sp_spot.append(lambda e: e.wait_ge(lo_made, n - N_RAW + 1))
        src = dram["pack_" + key][at:at + P * size].rearrange("(p f) -> p f", p=P)
        sp_spot.append(lambda e: e.dma_start(raw[:, 0:size], src).then_inc(raw_sem, 16))
        act_spot.append(lambda e: e.wait_ge(raw_sem, 16 * raw_n))
        if n >= N_SPLIT:
            used = panel_end[n - N_SPLIT]
            act_spot.append(lambda e: e.wait_ge(*used))
        act_spot.append(lambda e: e.activation(hi[:, 0:size], raw[:, 0:size], ACT.Copy).then_inc(hi_made, 1))
        dve_spot.append(lambda e: e.wait_ge(hi_made, n + 1))
        dve_spot.append(lambda e: e.tensor_tensor(
            lo[:, 0:size], raw[:, 0:size], hi[:, 0:size].bitcast(F32), ALU.subtract).then_inc(lo_made, 1))
        panel_n[0] += 1
        leave_spot()
        pe.items.append(lambda e: e.wait_ge(lo_made, n + 1))
        view = lambda t: t[:, 0:size].rearrange("p (k n) -> p k n", k=nk)
        return view(hi), view(lo), nk, width

    def end_panel():
        panel_end.append(pe.last())
        return pe.last()

    def products(out, pairs, after=(), signal=True, start=True, stop=True):
        pe.wait(after)
        todo = []
        for (lh, ll), (rh, rl) in pairs:
            todo += [(lh, rh), (lh, rl), (ll, rh)]
        token = None
        for n, (a, b) in enumerate(todo):
            last = n == len(todo) - 1
            issue = lambda e, a=a, b=b, n=n, last=last: e.matmul(out, a, b, start=(start and n == 0),
                                                                              stop=(stop and last))
            token = pe.op(issue, signal=signal and last)
        return token

    def mm(out, lhs, rhs, start=True, stop=True, after=(), signal=True):
        return pe.op(lambda e: e.matmul(out, lhs, rhs, start=start, stop=stop), after, signal)

    def transpose(out, in_, after=(), signal=True):
        return pe.op(lambda e: e.transpose(out, in_, const("ident")), after, signal)

    def split(hi, lo, src, after):
        a = act.op(lambda e: e.activation(hi, src, ACT.Copy), after)
        b = dve.op(lambda e: e.tensor_tensor(lo, src, hi.bitcast(F32), ALU.subtract), [a])
        return b

    def gemm_steps(key, block, act_hi, act_lo, tokens, ready, evacuate, token_major=False, panels=None):
        first, last = panels or (0, len(where[key][block]))
        for i in range(first, last):
            hi, lo, nk, width = panel(key, block, i)
            if token_major:
                todo = [[m] for m in range(tokens // P)]
            elif i == first and width == 2 * P:
                todo = [[0, 1]]
            else:
                todo = [[c] for c in range(width // P)]
            for group in todo:
                taken = [gemm_banks.take() for _ in group]
                for _, _, free in taken:
                    pe.wait(free)
                toks = []
                for k in range(nk):
                    pe.wait([ready(k)])
                    for (b, bank, _), m in zip(taken, group):
                        cut = slice(m * P, (m + 1) * P)
                        if token_major:
                            out = bank[:, 0:width]
                            left, right = (act_hi[:, k, cut], act_lo[:, k, cut]), (hi[:, k, :], lo[:, k, :])
                        else:
                            out = bank[:, 0:tokens]
                            left, right = (hi[:, k, cut], lo[:, k, cut]), (act_hi[:, k, 0:tokens],
                                                                           act_lo[:, k, 0:tokens])
                        tok = products(out, [(left, right)], signal=(k == nk - 1), start=(k == 0), stop=(k == nk - 1))
                        if k == nk - 1:
                            toks.append(tok)
                    yield
                if group[-1] == todo[-1][-1]:
                    end_panel()
                for (b, bank, _), m, tok in zip(taken, group, toks):
                    if token_major:
                        gemm_banks.give(b, *evacuate(i, m, bank[:, 0:width], tok))
                    else:
                        gemm_banks.give(b, *evacuate((i - first) * (PW // P) + m, bank[:, 0:tokens], tok))
                    for _ in range(background_pace[0]):
                        next(background[0], None)

    background = [iter(())]
    background_pace = [0]

    def gemm(*args, **kw):
        for _ in gemm_steps(*args, **kw):
            pass

    got_prm = load(prm[:, :], dram["params"], queue=act)
    consts_in = dram["consts"].rearrange("p (n f) -> p n f", n=len(CONSTS))
    got_cst = load(kept_consts[:, :, :], consts_in[:, 0:N_KEPT, :], queue=act)
    got_x = load(x_t[:, :, :], dram["x_t"].rearrange("(k p) t -> p k t", p=P), queue=act)
    for q in engines:
        q.wait([got_prm, got_cst, got_x])
    leave_spot()

    stat_bank = banks[7]
    stat_free = [()]
    rstd_free = [()]
    x_tok = {}

    class SquareSum:

        def __init__(self, n_tiles, tokens, out, free):
            self.n_tiles, self.tokens, self.k = n_tiles, tokens, 0
            self.out, self.free, self.token = out, list(free), None

        def add(self, src, after, behind=False):
            if self.k == 0:
                self.token = act.op(lambda e: e.activation(self.out, src, ACT.Square), self.free + list(after))
            else:
                i, buf, rd = tmps.take()
                buf = buf[:, 0:self.tokens]
                s = act.op(lambda e: e.activation(buf, src, ACT.Square), list(rd) + list(after))
                q = pool if behind and self.k < self.n_tiles - 1 else dve
                self.token = q.op(lambda e: e.tensor_tensor(self.out, self.out, buf, ALU.add), [s, self.token])
                tmps.give(i, self.token)
            self.k += 1

        def finish(self, eps="eps"):
            assert self.k == self.n_tiles
            bank = stat_bank[:, 0:self.tokens]
            t = mm(bank, const("ones"), self.out, after=[self.token] + list(stat_free[0]))
            a = act.op(lambda e: e.activation(self.out, bank, ACT.Sqrt, bias=param(eps),
                                              scale=1.0 / (self.n_tiles * P)), [t])
            stat_free[0] = (a,)
            return dve.op(lambda e: e.reciprocal(self.out, self.out), [a])

    next_sum = [None]

    def x_written(n, token):
        x_tok[n] = token
        if next_sum[0] is not None:
            next_sum[0].add(x_t[:, n, :], [token], behind=True)

    def prepare_sum():
        next_sum[0] = SquareSum(DT, T, rstd[:, :], rstd_free[0])

    def rstd_of_x():
        total, next_sum[0] = next_sum[0], None
        r = total.finish()
        return r

    def norm_to_h(src, gain, shift, tokens, hi, lo, r, src_ready):
        readers = [pe.last()]
        toks = []
        for k in range(DT):
            i, y, rd = tmps.take()
            y = y[:, 0:tokens]
            t = dve.op(lambda e, k=k, y=y: e.scalar_tensor_tensor(
                out=y, in0=src(k), scalar=gain(k), in1=rstd[:, 0:tokens],
                op0=ALU.mult, op1=ALU.mult), list(rd) + [r] + src_ready(k))
            if shift is None:
                t2 = split(hi[:, k, 0:tokens], lo[:, k, 0:tokens], y, [t] + readers)
            else:
                h, l = hi[:, k, 0:tokens], lo[:, k, 0:tokens]
                a = act.op(lambda e, y=y, h=h, k=k: e.activation(h, y, ACT.Identity, bias=shift(k)), [t] + readers)
                t2 = dve.op(lambda e, y=y, h=h, l=l, k=k: e.scalar_tensor_tensor(
                    out=l, in0=y, scalar=shift(k), in1=h.bitcast(F32), op0=ALU.add, op1=ALU.subtract), [a])
            tmps.give(i, t2)
            toks.append(t2)
        rstd_free[0] = (t,)
        return toks

    def norm_x(gain, shift=None):
        r = rstd_of_x()
        return norm_to_h(lambda k: x_t[:, k, :], gain, shift, T, h_hi, h_lo, r, lambda k: [x_tok.get(k)])

    def norm_other(src, gain, shift, tokens, hi, lo):
        total = SquareSum(DT, tokens, rstd[:, 0:tokens], rstd_free[0])
        for k in range(DT):
            total.add(src(k), [])
        r = total.finish()
        return norm_to_h(src, gain, shift, tokens, hi, lo, r, lambda k: [])

    def mixer():
        outer = ExitStack()
        prepare_sum()
        for k in range(DT):
            next_sum[0].add(x_t[:, k, :], [])
        h_ready = norm_x(lambda k: param("norm_mix_g", k, k + 1))
        ready = lambda k: h_ready[k]
        lgate = sb(outer, "lgate", [16, T])
        o_t = sb(outer, "heads_t", [P, DT, T])
        with ExitStack() as st2:
            gdn(st2, o_t, ready, lgate)
            fence()
        merged = sb(outer, "merged", [P, DT, T])
        with ExitStack() as st:
            o_hi = sb(st, "oa_hi", [P, DT, T], F32R)
            o_lo = sb(st, "oa_lo", [P, DT, T], F32R)
            gated_norm(st, "oa", o_t, 1, GDN_H, "gdn_norm_g", "gdn_z", ready, o_hi, o_lo)
            gate_and_branch(st, "a", "gate_a", "branch_a", ready, o_hi, o_lo, merged, True)
            fence()
        with ExitStack() as st:
            with ExitStack() as st2:
                gla(st2, o_t, ready, lgate)
                fence()
            o_hi = sb(st, "ob_hi", [P, DT, T], F32R)
            o_lo = sb(st, "ob_lo", [P, DT, T], F32R)
            gated_norm(st, "ob", o_t, 2, GLA_H, "gla_norm_g", "gla_r", ready, o_hi, o_lo)
            gate_and_branch(st, "b", "gate_b", "branch_b", ready, o_hi, o_lo, merged, False)
            fence()
        m_ready = []
        h_free = pe.last()
        for k in range(DT):
            t = dve.op(lambda e, k=k: e.tensor_scalar(merged[:, k, :], merged[:, k, :], 0.5, None, ALU.mult))
            m_ready.append(split(h_hi[:, k, :], h_lo[:, k, :], merged[:, k, :], [t, h_free]))
        prepare_sum()
        gemm("w_out", 0, h_hi, h_lo, T, lambda k: m_ready[k], add_to_x)
        outer.close()

    def add_to_x(n, ps, tok):
        t = dve.op(lambda e: e.tensor_tensor(x_t[:, n, :], x_t[:, n, :], ps, ALU.add), [tok, x_tok.get(n)])
        x_written(n, t)
        return [t]

    def gated_norm(st, name, o, tiles, heads, gain, key, ready, o_hi, o_lo):
        normed = []
        for h in range(heads):
            i, r, rd = tmps.take()
            total = SquareSum(tiles, T, r[:, :], rd)
            for j in range(tiles):
                total.add(o[:, h * tiles + j, :], [])
            t = total.finish()
            for j in range(tiles):
                k = h * tiles + j
                t2 = dve.op(lambda e, k=k, j=j, r=r: e.scalar_tensor_tensor(
                    out=o[:, k, :], in0=o[:, k, :], scalar=param(gain, j, j + 1), in1=r[:, :],
                    op0=ALU.mult, op1=ALU.mult), [t])
                normed.append(t2)
            tmps.give(i, t2)
        done = {}

        def take_z(n, ps, tok):
            i, z, rd = tmps.take()
            a = act.op(lambda e: e.activation(z[:, :], ps, ACT.Tanh, scale=0.5), [tok] + list(rd))
            t = dve.op(lambda e: e.scalar_tensor_tensor(out=z[:, :], in0=z[:, :], scalar=1.0, in1=ps,
                                                        op0=ALU.add, op1=ALU.mult), [a])
            t2 = dve.op(lambda e: e.scalar_tensor_tensor(out=z[:, :], in0=z[:, :], scalar=0.5, in1=o[:, n, :],
                                                         op0=ALU.mult, op1=ALU.mult), [t, normed[n]])
            done[n] = split(o_hi[:, n, :], o_lo[:, n, :], z[:, :], [t2])
            tmps.give(i, done[n])
            return [t]

        gemm(key, 0, h_hi, h_lo, T, ready, take_z)
        o_ready.clear()
        o_ready.update(done)

    o_ready = {}

    def gate_and_branch(st, name, gate_key, branch_key, ready, o_hi, o_lo, merged, first):
        g = sb(st, f"gate_{name}", [P, DT, T])
        g_ready = {}

        def take_gate(n, ps, tok):
            g_ready[n] = act.op(lambda e: e.activation(g[:, n, :], ps, ACT.Tanh, scale=0.5), [tok])
            return [g_ready[n]]

        gemm(gate_key, 0, h_hi, h_lo, T, ready, take_gate)
        branch_ready = dict(o_ready)

        def take_branch(n, ps, tok):
            dst = merged[:, n, :] if first else g[:, n, :]
            t = dve.op(lambda e: e.scalar_tensor_tensor(out=dst, in0=g[:, n, :], scalar=1.0, in1=ps,
                                                        op0=ALU.add, op1=ALU.mult), [tok, g_ready[n]])
            if not first:
                dve.op(lambda e: e.tensor_tensor(merged[:, n, :], merged[:, n, :], g[:, n, :], ALU.add), [t])
            return [t]

        gemm(branch_key, 0, o_hi, o_lo, T, lambda k: branch_ready[k], take_branch)

    def softplus_parts(st, name, z, shape, ready):
        a = sb(st, f"{name}_abs", shape)
        flat = a[:, :]
        t = act.op(lambda e: e.activation(flat, z, ACT.Abs), [ready])
        t = act.op(lambda e: e.activation(flat, flat, ACT.Exp, scale=-1.0), [t])
        t = act.op(lambda e: e.activation(flat, flat, ACT.Ln, bias=1.0), [t])
        return a, t

    def gdn(st, q_t, ready, lgate):
        scan_consts.append(sb(st, "scan_consts", [P, len(CONSTS) - N_KEPT, P]))
        got = load(scan_consts[0][:, :, :], consts_in[:, N_KEPT:, :])
        for q in (pe, dve, pool):
            q.wait([got])
        k_t = sb(st, "k_t", [P, GDN_H, T])
        v_t = sb(st, "v_t", [P, GDN_H, T])
        gb = sb(st, "gdn_gb", [P, NCH * 16])
        gbv = gb[:, :].rearrange("p (c n) -> p c n", c=NCH)
        beta = sb(st, "beta", [P, NCH * 8])
        g = sb(st, "gdn_g", [P, NCH * 8])
        z = sb(st, "gdn_zg", [P, NCH * 8])
        neg_a = sb(st, "neg_a", [P, 8])

        hi, lo, nk, width = panel("gates", 0, 0)
        toks = []
        b, bank, free = gemm_banks.take()
        for c in range(NCH):
            cut = slice(c * P, (c + 1) * P)
            t = products(bank[:, c * 16:(c + 1) * 16],
                         [((h_hi[:, k, cut], h_lo[:, k, cut]), (hi[:, k, 0:16], lo[:, k, 0:16])) for k in range(nk)],
                         after=list(free) + [ready(k) for k in range(nk)])
        t = act.op(lambda e, bank=bank: e.activation(gb[:, :], bank[:, 0:NCH * 16], ACT.Copy), [t])
        gemm_banks.give(b, t)
        b, bank, free = gemm_banks.take()
        products(bank[0:16, :], [((hi[:, k, 16:32], lo[:, k, 16:32]), (h_hi[:, k, :], h_lo[:, k, :]))
                                 for k in range(nk)], after=free)
        tl = end_panel()
        tl = act.op(lambda e, bank=bank: e.activation(lgate[:, :], bank[0:16, :], ACT.Copy), [tl])
        gemm_banks.give(b, tl)

        v3 = lambda tile: tile[:, :].rearrange("p (c n) -> p c n", c=NCH)
        bc = lambda ap: ap[:, None, :].to_broadcast([P, NCH, 8])
        tb = act.op(lambda e: e.activation(v3(beta), gbv[:, :, 8:16], ACT.Tanh, scale=0.5), [t])
        tb = dve.op(lambda e: e.tensor_scalar(beta[:, :], beta[:, :], 0.5, 0.5, ALU.mult, ALU.add), [tb])
        tz = dve.op(lambda e: e.tensor_tensor(v3(z), gbv[:, :, 0:8], bc(param("dt_bias")), ALU.add), [t])
        ta = act.op(lambda e: e.activation(neg_a[:, :], param("a_log"), ACT.Exp))
        sp_tile, ts = softplus_parts(st, "gdn_sp", z[:, :], [P, NCH * 8], tz)
        tz = dve.op(lambda e: e.scalar_tensor_tensor(out=z[:, :], in0=z[:, :], scalar=0.0, in1=sp_tile[:, :],
                                                     op0=ALU.max, op1=ALU.add), [ts])
        tz = dve.op(lambda e: e.scalar_tensor_tensor(out=v3(g), in0=v3(z), scalar=-1.0, in1=bc(neg_a[:, :]),
                                                     op0=ALU.mult, op1=ALU.mult), [tz, ta])
        g_ready = tz

        with ExitStack() as cs:
            raws = [sb(cs, f"conv_in{i}", [P, T + 4]) for i in range(2)]
            pads = [pool.op(lambda e, r=r: e.memset(r[:, 0:3], 0.0)) for r in raws]
            raw_ring = Ring(raws)
            raw_ring.free = [(p,) for p in pads]
            tanhs = tmps
            made = {}

            def conv(n, ps, tok):
                i, raw, rd = raw_ring.take()
                a = act.op(lambda e: e.activation(raw[:, 3:3 + T], ps, ACT.Copy), [tok] + list(rd))
                dst = (q_t, k_t, v_t)[n // GDN_H][:, n % GDN_H, :]
                w = lambda j: param("gdn_conv_w", n * 4 + j, n * 4 + j + 1)
                t = dve.op(lambda e: e.tensor_scalar(dst, raw[:, 0:T], w(0), None, ALU.mult), [a])
                for j in range(1, 4):
                    t = dve.op(lambda e, j=j: e.scalar_tensor_tensor(
                        out=dst, in0=raw[:, j:j + T], scalar=w(j), in1=dst, op0=ALU.mult, op1=ALU.add), [t])
                raw_ring.give(i, t)
                i2, th, rd2 = tanhs.take()
                s = act.op(lambda e: e.activation(th[:, :], dst, ACT.Tanh, scale=0.5), [t] + list(rd2))
                t = dve.op(lambda e: e.scalar_tensor_tensor(out=dst, in0=th[:, :], scalar=1.0, in1=dst,
                                                            op0=ALU.add, op1=ALU.mult), [s])
                tanhs.give(i2, t)
                made[n] = t
                return [a]

            gemm("gdn_qkv", 0, h_hi, h_lo, T, ready, conv)
            inv = sb(cs, "l2_inverse", [P, 2 * GDN_H, NCH])
            ib, inv_bank, inv_free = work_banks.take()
            inv_psum = inv_bank[:, 0:2 * GDN_H * NCH].rearrange("p (n c) -> p n c", c=NCH)
            for n in range(2 * GDN_H):
                tile = (q_t, k_t)[n // GDN_H][:, n % GDN_H, :]
                i, sqb, rd = tmps.take()
                s = act.op(lambda e, tile=tile, sqb=sqb: e.activation(sqb[:, :], tile, ACT.Square),
                           [made[n]] + list(rd))
                for c in range(NCH):
                    tok = mm(inv_psum[:, n, c:c + 1], sqb[:, c * P:(c + 1) * P], const("ones")[:, 0:1],
                             after=[s] + list(inv_free), signal=(c == NCH - 1))
                tmps.give(i, tok)
            s = act.op(lambda e: e.activation(inv[:, :, :], inv_psum, ACT.Sqrt, bias=param("eps4")), [tok])
            work_banks.give(ib, s)
            t_inv = dve.op(lambda e: e.reciprocal(inv[:, :, :], inv[:, :, :]), [s])
            for n in range(2 * GDN_H):
                tile = (q_t, k_t)[n // GDN_H][:, n % GDN_H, :]
                i, diag, rd = tmps.take()
                q = (pool, dve)[n % 2]
                t = q.op(lambda e, n=n, diag=diag: e.tensor_tensor(
                    diag[:, :].rearrange("p (c i) -> p c i", c=NCH),
                    const("ident")[:, None, :].to_broadcast([P, NCH, P]),
                    inv[:, n, :][:, :, None].to_broadcast([P, NCH, P]), ALU.mult), [t_inv] + list(rd))
                b, bank, free = work_banks.take()
                tok = mm(bank[:, :], const("ones"), diag[:, :], after=[t] + list(free))
                tmps.give(i, tok)
                scale = P ** -0.5 if n < GDN_H else 1.0
                t = dve.op(lambda e, tile=tile, bank=bank, scale=scale: e.scalar_tensor_tensor(
                    out=tile, in0=tile, scalar=scale, in1=bank[:, :], op0=ALU.mult, op1=ALU.mult), [tok])
                work_banks.give(b, t)
            fence()

        W4 = [P, 4, P]
        scan_banks = Ring(banks[0:7])
        flat = lambda ap: ap.rearrange("p a b -> p (a b)")
        bank4 = lambda bank: bank[:, :].rearrange("p (h f) -> p h f", h=4)
        mask4 = lambda name: const(name)[:, None, :].to_broadcast(W4)
        gv = v3(g)
        bv3 = v3(beta)
        state = sb(st, "gdn_state", [P, GDN_H, P])

        def group_of_heads(grp):
            names = ("g_u", "e_row", "e_mat", "e_mat_t", "low", "low_t", "dd", "dd_t", "pp", "off_t", "kb", "a_t")
            own = 12 if grp == 0 else 7
            tiles = [sb(st, f"{name}_{grp}", W4) for name in names[0:own]]
            tiles += [idle[:, :].rearrange("p (a b) -> p a b", a=4) for idle in (tmp_tiles + [rstd])[0:12 - own]]
            g_u, e_row, e_mat, e_mat_t, low, low_t, dd, dd_t, pp, off_t, kb, a_t = tiles
            cols = sb(st, f"gdn_cols_{grp}", [P, 4, 8])
            b_v, kbg, kdec, w_t, u_m, delta, q_dec = e_mat, low, off_t, pp, low_t, dd, g_u
            chunk_before = []
            for c in range(NCH):
                tok_cut = slice(c * P, (c + 1) * P)
                yield
                b, bank, free = scan_banks.take()
                mm(bank[:, 0:8], const("incl_t"), gv[:, c, :], after=list(free) + [g_ready], signal=False)
                t = mm(bank[:, 8:16], const("strict"), gv[:, c, :])
                t = act.op(lambda e, bank=bank: e.activation(cols[:, 0:2, :], bank[:, 0:16].rearrange(
                    "p (a h) -> p a h", a=2), ACT.Exp), [t] + chunk_before)
                scan_banks.give(b, t)
                t = dve.op(lambda e, c=c: e.tensor_tensor(cols[:, 2, :], cols[:, 0, :], bv3[:, c, :], ALU.mult), [t])
                t_cols = dve.op(lambda e, c=c: e.tensor_scalar(cols[:, 3, :], bv3[:, c, :], 0.5, None, ALU.mult), [t])
                hs = slice(4 * grp, 4 * grp + 4)
                col4 = lambda r, grp=grp: cols[:, r, 4 * grp:4 * grp + 4][:, :, None].to_broadcast(W4)
                t = dve.op(lambda e, c=c, grp=grp: e.tensor_tensor(
                    g_u[:, :, :], mask4("incl_t"),
                    gv[:, c, 4 * grp:4 * grp + 4][:, :, None].to_broadcast(W4), ALU.mult), chunk_before)
                t_gu = t
                yield
                b, bank, free = scan_banks.take()
                t = mm(bank[:, :], const("ones"), flat(g_u[:, :, :]), after=[t_gu] + list(free))
                t_er = act.op(lambda e, bank=bank: e.activation(flat(e_row[:, :, :]), bank[:, :], ACT.Exp), [t])
                scan_banks.give(b, t_er)
                yield
                b, bank, free = scan_banks.take()
                for h in range(4):
                    t = mm(bank4(bank)[:, h, :], g_u[:, h, :], const("strict"), after=free, signal=(h == 3))
                t_e = act.op(lambda e, bank=bank: e.activation(flat(e_mat[:, :, :]), bank[:, :], ACT.Exp), [t])
                scan_banks.give(b, t_e)
                yield
                b, bank, free = scan_banks.take()
                t_gu_read = mm(bank[:, :], const("strict"), flat(g_u[:, :, :]), after=free)
                t_et = act.op(lambda e, bank=bank: e.activation(flat(e_mat_t[:, :, :]), bank[:, :], ACT.Exp),
                              [t_gu_read])
                scan_banks.give(b, t_et)
                t = dve.op(lambda e, c=c, grp=grp: e.tensor_tensor(
                    pp[:, :, :], mask4("ident"),
                    bv3[:, c, 4 * grp:4 * grp + 4][:, :, None].to_broadcast(W4), ALU.mult))
                yield
                b, bank, free = scan_banks.take()
                t = mm(bank[:, :], const("ones"), flat(pp[:, :, :]), after=[t] + list(free))
                t_kb = dve.op(lambda e, bank=bank, hs=hs, cut=tok_cut: e.tensor_tensor(
                    kb[:, :, :], k_t[:, hs, cut], bank4(bank), ALU.mult), [t])
                scan_banks.give(b, t_kb)
                yield
                b, bank, free = scan_banks.take()
                for h in range(4):
                    t = mm(bank4(bank)[:, h, :], kb[:, h, :], k_t[:, 4 * grp + h, tok_cut],
                           after=[t_kb] + list(free), signal=(h == 3))
                tm = pool.op(lambda e: e.tensor_tensor(e_mat[:, :, :], e_mat[:, :, :], mask4("strict"), ALU.mult),
                             [t_e])
                t_low = dve.op(lambda e, bank=bank: e.tensor_tensor(flat(low[:, :, :]), flat(e_mat[:, :, :]),
                                                                    bank[:, :], ALU.mult), [t, tm])
                scan_banks.give(b, t_low)
                yield
                b, bank, free = scan_banks.take()
                for h in range(4):
                    t = mm(bank4(bank)[:, h, :], k_t[:, 4 * grp + h, tok_cut], kb[:, h, :], after=free,
                           signal=(h == 3))
                tm = pool.op(lambda e: e.tensor_tensor(low_t[:, :, :], e_mat_t[:, :, :], mask4("strict_t"), ALU.mult),
                             [t_et])
                t_lt = dve.op(lambda e, bank=bank: e.tensor_tensor(flat(low_t[:, :, :]), flat(low_t[:, :, :]),
                                                                   bank[:, :], ALU.mult), [t, tm])
                scan_banks.give(b, t_lt)
                yield
                b, bank, free = scan_banks.take()
                for h in range(4):
                    t = mm(bank4(bank)[:, h, :], k_t[:, 4 * grp + h, tok_cut], q_t[:, 4 * grp + h, tok_cut],
                           after=free, signal=(h == 3))
                tm = pool.op(lambda e: e.tensor_tensor(e_mat_t[:, :, :], e_mat_t[:, :, :], mask4("incl_t"), ALU.mult),
                             [tm])
                t_a = dve.op(lambda e, bank=bank: e.tensor_tensor(flat(a_t[:, :, :]), flat(e_mat_t[:, :, :]),
                                                                  bank[:, :], ALU.mult), [t, tm])
                scan_banks.give(b, t_a)
                t_qd = pool.op(lambda e, hs=hs, cut=tok_cut: e.tensor_tensor(
                    q_dec[:, :, :], q_t[:, hs, cut], e_row[:, :, :], ALU.mult), [t_er, t_gu_read, t_a])

                t = pool.op(lambda e: e.tensor_tensor(dd[:, :, :], low[:, :, :], mask4("lvl1"), ALU.mult), [t_low])
                t_d = dve.op(lambda e: e.tensor_tensor(dd[:, :, :], mask4("ident"), dd[:, :, :], ALU.subtract), [t])
                t = pool.op(lambda e: e.tensor_tensor(dd_t[:, :, :], low_t[:, :, :], mask4("lvl1_t"), ALU.mult),
                            [t_lt])
                t_dt = dve.op(lambda e: e.tensor_tensor(dd_t[:, :, :], mask4("ident"), dd_t[:, :, :], ALU.subtract),
                              [t])
                t_p_read = None
                for s in (2, 4, 8, 16, 32, 64):
                    t_o = pool.op(lambda e, s=s: e.tensor_tensor(off_t[:, :, :], low_t[:, :, :],
                                                                 mask4(f"lvl{s}_t"), ALU.mult), [t_lt, t_p_read])
                    yield
                    b, bank, free = scan_banks.take()
                    for h in range(4):
                        t = mm(bank4(bank)[:, h, :], off_t[:, h, :], dd[:, h, :], after=[t_o, t_d] + list(free),
                               signal=(h == 3))
                    t_p_read = t
                    t_p = act.op(lambda e, bank=bank: e.activation(flat(pp[:, :, :]), bank[:, :], ACT.Copy), [t])
                    scan_banks.give(b, t_p)
                    if s < 64:
                        yield
                        b, bank, free = scan_banks.take()
                        for h in range(4):
                            t = mm(bank4(bank)[:, h, :], dd_t[:, h, :], pp[:, h, :], after=[t_p, t_dt] + list(free),
                                   signal=(h == 3))
                        t_d = dve.op(lambda e, bank=bank: e.tensor_tensor(
                            flat(dd[:, :, :]), flat(dd[:, :, :]), bank[:, :], ALU.subtract), [t])
                        scan_banks.give(b, t_d)
                    yield
                    b, bank, free = scan_banks.take()
                    for h in range(4):
                        t = mm(bank4(bank)[:, h, :], pp[:, h, :], dd_t[:, h, :], after=[t_p, t_dt] + list(free),
                               signal=(h == 3))
                    t_dt = dve.op(lambda e, bank=bank: e.tensor_tensor(
                        flat(dd_t[:, :, :]), flat(dd_t[:, :, :]), bank[:, :], ALU.subtract), [t])
                    scan_banks.give(b, t_dt)

                yield
                b, bank, free = scan_banks.take()
                for h in range(4):
                    t = transpose(bank4(bank)[:, h, :], k_t[:, 4 * grp + h, tok_cut], after=free, signal=(h == 3))
                t_kbg = dve.op(lambda e, bank=bank, col4=col4: e.tensor_tensor(
                    kbg[:, :, :], bank4(bank), col4(2), ALU.mult), [t, t_low, t_cols, t_dt])
                t_kd = dve.op(lambda e, bank=bank, col4=col4: e.tensor_tensor(
                    kdec[:, :, :], bank4(bank), col4(1), ALU.mult), [t_kbg])
                scan_banks.give(b, t_kd)
                yield
                b, bank, free = scan_banks.take()
                for h in range(4):
                    t = transpose(bank4(bank)[:, h, :], v_t[:, 4 * grp + h, tok_cut], after=free, signal=(h == 3))
                t_bv = dve.op(lambda e, bank=bank, col4=col4: e.tensor_tensor(
                    b_v[:, :, :], bank4(bank), col4(3), ALU.mult), [t, t_low])
                scan_banks.give(b, t_bv)
                yield
                b, bank, free = scan_banks.take()
                for h in range(4):
                    t = mm(bank4(bank)[:, h, :], dd_t[:, h, :], b_v[:, h, :], after=[t_bv, t_dt] + list(free),
                           signal=(h == 3))
                t_u = act.op(lambda e, bank=bank: e.activation(flat(u_m[:, :, :]), bank[:, :], ACT.Copy), [t])
                scan_banks.give(b, t_u)
                if c == 0:
                    delta_now, t_del = u_m, t_u
                else:
                    yield
                    b, bank, free = scan_banks.take()
                    for h in range(4):
                        t = mm(bank4(bank)[:, h, :], kbg[:, h, :], dd_t[:, h, :], after=[t_kbg] + list(free),
                               signal=(h == 3))
                    t_w = act.op(lambda e, bank=bank: e.activation(flat(w_t[:, :, :]), bank[:, :], ACT.Copy), [t])
                    scan_banks.give(b, t_w)
                    yield
                    b, bank, free = scan_banks.take()
                    for h in range(4):
                        t = mm(bank4(bank)[:, h, :], w_t[:, h, :], state[:, 4 * grp + h, :],
                               after=[t_w] + list(free), signal=(h == 3))
                    t_del = dve.op(lambda e, bank=bank: e.tensor_tensor(
                        flat(delta[:, :, :]), flat(u_m[:, :, :]), bank[:, :], ALU.subtract), [t, t_u, t_d])
                    scan_banks.give(b, t_del)
                    delta_now = delta
                yield
                b, bank, free = scan_banks.take()
                for h in range(4):
                    if c > 0:
                        mm(bank4(bank)[:, h, :], state[:, 4 * grp + h, :], q_dec[:, h, :], stop=False,
                           after=[t_qd] + list(free), signal=False)
                    t = mm(bank4(bank)[:, h, :], delta_now[:, h, :], a_t[:, h, :], start=(c == 0),
                           after=[t_del, t_a, t_qd] + list(free), signal=(h == 3))
                t_o = act.op(lambda e, bank=bank, hs=hs, cut=tok_cut: e.activation(
                    q_t[:, hs, cut], bank4(bank), ACT.Copy), [t])
                scan_banks.give(b, t_o)
                if c < NCH - 1:
                    yield
                    b, bank, free = scan_banks.take()
                    for h in range(4):
                        t = mm(bank4(bank)[:, h, :], kdec[:, h, :], delta_now[:, h, :], after=[t_kd] + list(free),
                               signal=(h == 3))
                    if c == 0:
                        t = act.op(lambda e, bank=bank, hs=hs: e.activation(state[:, hs, :], bank4(bank), ACT.Copy),
                                   [t])
                    else:
                        ts = dve.op(lambda e, hs=hs: e.tensor_tensor(
                            state[:, hs, :], state[:, hs, :], e_row[:, :, P - 1:P].to_broadcast(W4), ALU.mult), [t])
                        t = dve.op(lambda e, bank=bank, hs=hs: e.tensor_tensor(
                            state[:, hs, :], state[:, hs, :], bank4(bank), ALU.add), [ts])
                    scan_banks.give(b, t)
                chunk_before = everything()

        running = [group_of_heads(0), group_of_heads(1)]
        while running:
            for steps in list(running):
                if next(steps, "end") == "end":
                    running.remove(steps)

    def gla(st, o_t, ready, lgate):
        q = sb(st, "gla_q", [P, GLA_H, T])
        k = sb(st, "gla_k", [P, GLA_H, T])
        v = sb(st, "gla_v", [P, NCH, D])
        w2 = sb(st, "gla_w2", [16, 512])
        bc_sum = sb(st, "gla_bc", [P, T])
        lf = sb(st, "gla_lf", [P, T])
        e_q, kd = q, k
        q_in = sb(st, "gla_qin", [P, T])
        k_in = sb(st, "gla_kin", [P, T])
        k_x = sb(st, "gla_kx", [P, NCH, 64])
        q_x = sb(st, "gla_qx", [P, NCH, 64])
        reset = sb(st, "gla_reset", [P, T])
        a_t = sb(st, "gla_at", [P, NCH, P])
        g_end = sb(st, "gla_gend", [P, GLA_H, NCH])
        t_w2 = load(w2[:, :], dram["gla_w2"], after=everything())
        r4 = reset[:, :].rearrange("p (c i) -> p c i", c=NCH)
        t_rs = pool.op(lambda e: e.memset(reset[:, :], 1.0))
        t_rs = pool.op(lambda e: e.memset(r4[:, :, 0:1], 0.0), [t_rs])
        t_az = pool.op(lambda e: e.memset(a_t[:, :, :], 0.0))
        made = {}

        def take_qk(n, ps, tok):
            dst = q[:, n, :] if n < GLA_H else k[:, n - GLA_H, :]
            made[n] = act.op(lambda e: e.activation(dst, ps, ACT.Copy, scale=P ** -0.5 if n < GLA_H else 1.0), [tok])
            return [made[n]]

        gemm("gla_qk", 0, h_hi, h_lo, T, ready, take_qk)

        def take_v(i, m, ps, tok):
            t = act.op(lambda e: e.activation(v[:, m, i * PW:(i + 1) * PW], ps, ACT.Copy), [tok])
            return [t]

        gemm("gla_v", 0, h_hi, h_lo, T, ready, take_v, token_major=True)
        t_v = act.last()

        c4 = lambda ap: ap.rearrange("p (c i) -> p c i", c=NCH)
        c8 = lambda ap: ap.rearrange("p (c i) -> p c i", c=2 * NCH)
        with ExitStack() as es:
            ex = sb(es, "gla_ex", [P, T])
            ab = sb(es, "gla_ab", [P, T])
            for h in range(GLA_H):
                b, bank, free = work_banks.take()
                t = mm(bank[:, :], w2[:, h * P:(h + 1) * P], lgate[:, :], after=[t_w2] + list(free))
                t = act.op(lambda e, bank=bank, h=h: e.activation(lf[:, :], bank[:, :], ACT.Identity,
                                                                  bias=param("gla_b_gate", h, h + 1)),
                           [t, dve.last()])
                work_banks.give(b, t)
                t = act.op(lambda e: e.activation(ab[:, :], lf[:, :], ACT.Abs), [t])
                t = act.op(lambda e: e.activation(ab[:, :], ab[:, :], ACT.Exp, scale=-1.0), [t])
                t = act.op(lambda e: e.activation(ab[:, :], ab[:, :], ACT.Ln, bias=1.0), [t])
                t = dve.op(lambda e: e.scalar_tensor_tensor(out=lf[:, :], in0=lf[:, :], scalar=0.0, in1=ab[:, :],
                                                            op0=ALU.min, op1=ALU.subtract), [t])
                t = dve.op(lambda e: e.tensor_scalar(lf[:, :], lf[:, :], 1.0 / GLA_TAU, None, ALU.mult), [t])
                t_bc = dve.op(lambda e: e.tensor_tensor_scan(bc_sum[:, :], reset[:, :], lf[:, :], 0.0,
                                                             ALU.mult, ALU.add), [t, t_rs])

                def decayed(dst, src, a, b_, shape, after):
                    exv = ex[:, 0:shape[1] * shape[2]].rearrange("p (c i) -> p c i", c=shape[1])
                    t = dve.op(lambda e: e.tensor_tensor(exv, a, b_, ALU.subtract), list(after) + [dve.last()])
                    t = act.op(lambda e: e.activation(exv, exv, ACT.Exp), [t])
                    return dve.op(lambda e: e.tensor_tensor(dst, src, exv, ALU.mult), [t])

                prev = [pe.last(), t_bc]
                s8, s4, sx = [P, 8, 64], [P, NCH, P], [P, NCH, 64]
                bc8, bc4 = c8(bc_sum[:, :]), c4(bc_sum[:, :])
                mid = bc8[:, :, 32:33].to_broadcast(s8)
                edge = bc4[:, :, 63:64].to_broadcast(sx)
                end = bc4[:, :, P - 1:P].to_broadcast(s4)
                decayed(c8(q_in[:, :]), c8(q[:, h, :]), bc8, mid, s8, prev + [made[h]])
                t_kin = decayed(c8(k_in[:, :]), c8(k[:, h, :]), mid, bc8, s8, [made[GLA_H + h]])
                decayed(q_x[:, :, :], c4(q[:, h, :])[:, :, 64:P], bc4[:, :, 64:P], edge, sx, [])
                t_x = decayed(k_x[:, :, :], c4(k[:, h, :])[:, :, 0:64], edge, bc4[:, :, 0:64], sx, [])
                t_kd = decayed(c4(kd[:, h, :]), c4(k[:, h, :]), end, bc4, s4, [])
                t = act.op(lambda e: e.activation(ex[:, :], bc_sum[:, :], ACT.Exp), [t_kd])
                dve.op(lambda e, h=h: e.tensor_tensor(e_q[:, h, :], q[:, h, :], ex[:, :], ALU.mult), [t])
                t_ge = dve.op(lambda e, h=h: e.tensor_copy(g_end[:, h, :], c4(ex[:, :])[:, :, P - 1]), [t])
                b, bank, free = work_banks.take()
                b4 = bank[:, :].rearrange("p (c i) -> p c i", c=NCH)
                for c in range(NCH):
                    o = c * P
                    mm(b4[0:64, c, 0:64], k_in[:, o:o + 64], q_in[:, o:o + 64],
                       after=[t_kin, t_x] + list(free), signal=False)
                    mm(b4[0:64, c, 64:P], k_x[:, c, :], q_x[:, c, :], signal=False)
                for c in range(NCH):
                    o = c * P
                    t = mm(b4[64:P, c, 64:P], k_in[:, o + 64:o + P], q_in[:, o + 64:o + P], signal=(c == NCH - 1))
                m4 = const("incl_t")[:, None, :].to_broadcast([P, NCH, P])
                t1 = dve.op(lambda e, b4=b4: e.tensor_tensor(a_t[0:64, :, :], b4[0:64, :, :], m4[0:64, :, :],
                                                             ALU.mult), [t, t_az])
                t_at = dve.op(lambda e, b4=b4: e.tensor_tensor(a_t[64:P, :, 64:P], b4[64:P, :, 64:P],
                                                               m4[64:P, :, 64:P], ALU.mult), [t1])
                work_banks.give(b, t_at)
                for eh in range(2):
                    b, bank, free = work_banks.take()
                    for c in range(NCH):
                        t = mm(bank[:, c * P:(c + 1) * P], v[:, c, (2 * h + eh) * P:(2 * h + eh + 1) * P],
                               a_t[:, c, :], after=[t_at, t_v] + list(free), signal=(c == NCH - 1))
                    t = act.op(lambda e, bank=bank, n=2 * h + eh: e.activation(o_t[:, n, :], bank[:, :], ACT.Copy),
                               [t])
                    work_banks.give(b, t)
            fence()

        state = sb(st, "gla_state", [P, GLA_H, 2 * P])
        kd_tm = sb(st, "gla_kdtm", [P, GLA_H, P])
        t_state = None
        for c in range(NCH):
            cut = slice(c * P, (c + 1) * P)
            if c > 0:
                for half in range(2):
                    b, bank, free = work_banks.take()
                    for j in range(4):
                        n = 4 * half + j
                        t = mm(bank[:, j * P:(j + 1) * P], state[:, n // 2, (n % 2) * P:(n % 2 + 1) * P],
                               e_q[:, n // 2, cut], after=[t_state] + list(free), signal=(j == 3))
                    t = dve.op(lambda e, bank=bank, half=half, cut=cut: e.tensor_tensor(
                        o_t[:, 4 * half:4 * half + 4, cut], o_t[:, 4 * half:4 * half + 4, cut],
                        bank[:, :].rearrange("p (n i) -> p n i", n=4), ALU.add), [t])
                    work_banks.give(b, t)
            if c < NCH - 1:
                b, bank, free = work_banks.take()
                for h in range(GLA_H):
                    t = transpose(bank[:, h * P:(h + 1) * P], kd[:, h, cut], after=free, signal=(h == GLA_H - 1))
                t_tm = act.op(lambda e, bank=bank: e.activation(kd_tm[:, :, :].rearrange("p h i -> p (h i)"),
                                                               bank[:, :], ACT.Copy), [t])
                work_banks.give(b, t_tm)
                for half in range(2):
                    b, bank, free = work_banks.take()
                    for j in range(2):
                        h = 2 * half + j
                        t = mm(bank[:, j * 256:(j + 1) * 256], kd_tm[:, h, :], v[:, c, h * 256:(h + 1) * 256],
                               after=[t_tm] + list(free), signal=(j == 1))
                    if c == 0:
                        t_state = dve.op(lambda e, bank=bank, half=half: e.tensor_copy(
                            state[:, 2 * half:2 * half + 2, :].rearrange("p h i -> p (h i)"), bank[:, :]), [t])
                    else:
                        for j in range(2):
                            h = 2 * half + j
                            t_state = dve.op(lambda e, bank=bank, h=h, j=j, c=c: e.scalar_tensor_tensor(
                                out=state[:, h, :], in0=state[:, h, :], scalar=g_end[:, h, c:c + 1],
                                in1=bank[:, j * 256:(j + 1) * 256], op0=ALU.mult, op1=ALU.add), [t])
                    work_banks.give(b, t_state)

    def cross_attention():
        with ExitStack() as outer:
            h_ready = norm_x(lambda k: param("norm_xattn_g", k, k + 1))
            fence()
            mk = sb(outer, "xk", [P, DT, MEM])
            mv = sb(outer, "xv", [P, 2, D])
            with ExitStack() as st:
                mem_t = sb(st, "mem_t", [P, DT, MEM])
                m_hi = sb(st, "m_hi", [P, DT, MEM], F32R)
                m_lo = sb(st, "m_lo", [P, DT, MEM], F32R)
                tm = load(mem_t[:, :, :], dram["mem_t"].rearrange("(k p) t -> p k t", p=P),
                          after=everything())
                act.wait([tm])
                dve.wait([tm])
                m_ready = norm_other(lambda k: mem_t[:, k, :], lambda k: param("norm_mem_g", k, k + 1),
                                     None, MEM, m_hi, m_lo)

                def take_k(n, ps, tok):
                    return [act.op(lambda e: e.activation(mk[:, n, :], ps, ACT.Copy), [tok])]

                def take_v(i, m, ps, tok):
                    return [act.op(lambda e: e.activation(mv[:, m, i * PW:(i + 1) * PW], ps, ACT.Copy), [tok])]

                gemm("xk", 0, m_hi, m_lo, MEM, lambda k: m_ready[k], take_k)
                gemm("xv", 0, m_hi, m_lo, MEM, lambda k: m_ready[k], take_v, token_major=True)
                fence()
            with ExitStack() as st:
                q = sb(st, "xq", [P, DT, T])

                def take_q(n, ps, tok):
                    return [act.op(lambda e: e.activation(q[:, n, :], ps, ACT.Copy), [tok])]

                gemm("xq", 0, h_hi, h_lo, T, lambda k: h_ready[k], take_q)
                t_q = act.last()
                pe.wait([t_q])
                scale = (D // XA_H) ** -0.5
                probs = Ring([sb(st, f"xp{i}", [P, 4, MEM]) for i in range(2)])
                pts = Ring([sb(st, f"xpt{i}", [P, 2, T]) for i in range(2)])
                stat = Ring([sb(st, f"xstat{i}", [P, 12]) for i in range(2)])
                ys = tmps
                o_rdy = {}
                for h in range(XA_H):
                    ip, p, rdp = probs.take()
                    is_, s, rds = stat.take()
                    for half in range(2):
                        b, bank, free = work_banks.take()
                        for j in range(2):
                            m = 2 * half + j
                            for kk in range(2):
                                t = mm(bank[:, j * MEM:(j + 1) * MEM], q[:, 2 * h + kk, m * P:(m + 1) * P],
                                       mk[:, 2 * h + kk, :], start=(kk == 0), stop=(kk == 1), after=free,
                                       signal=(j == 1 and kk == 1))
                        t = dve.op(lambda e, bank=bank, s=s, half=half: e.tensor_reduce(
                            s[:, 2 * half:2 * half + 2], bank[:, :].rearrange("p (a b) -> p a b", a=2), AX, ALU.max),
                            [t] + list(rds))
                        t = dve.op(lambda e, s=s, half=half: e.tensor_scalar(
                            s[:, 2 * half:2 * half + 2], s[:, 2 * half:2 * half + 2], -scale, None, ALU.mult), [t])
                        for j in range(2):
                            m = 2 * half + j
                            t = act.op(lambda e, bank=bank, s=s, p=p, m=m, j=j: e.activation(
                                p[:, m, :], bank[:, j * MEM:(j + 1) * MEM], ACT.Exp, bias=s[:, m:m + 1], scale=scale,
                                accum_out=s[:, 4 + m:5 + m]), [t] + list(rdp))
                        work_banks.give(b, t)
                    t = dve.op(lambda e, s=s: e.reciprocal(s[:, 8:12], s[:, 4:8]), [t])
                    t_p = dve.op(lambda e, s=s, p=p: e.tensor_tensor(
                        p[:, :, :], p[:, :, :], s[:, 8:12][:, :, None].to_broadcast([P, 4, MEM]), ALU.mult), [t])
                    stat.give(is_, t_p)
                    it, pt, rdt = pts.take()
                    for kt in range(2):
                        b, bank, free = work_banks.take()
                        for m in range(4):
                            t = transpose(bank[:, m * P:(m + 1) * P], p[:, m, kt * P:(kt + 1) * P],
                                          after=[t_p] + list(free), signal=(m == 3))
                        t2 = act.op(lambda e, bank=bank, pt=pt, kt=kt: e.activation(pt[:, kt, :], bank[:, :], ACT.Copy),
                                    [t] + list(rdt))
                        work_banks.give(b, t2)
                    probs.give(ip, t)
                    for eh in range(2):
                        n = 2 * h + eh
                        b, bank, free = work_banks.take()
                        for kt in range(2):
                            t = mm(bank[:, :], mv[:, kt, n * P:(n + 1) * P], pt[:, kt, :], start=(kt == 0),
                                   stop=(kt == 1), after=[t2] + list(free), signal=(kt == 1))
                        iy, y, rdy = ys.take()
                        ty = act.op(lambda e, bank=bank, y=y: e.activation(y[:, :], bank[:, :], ACT.Copy),
                                    [t] + list(rdy))
                        work_banks.give(b, ty)
                        o_rdy[n] = split(h_hi[:, n, :], h_lo[:, n, :], y[:, :], [ty])
                        ys.give(iy, o_rdy[n])
                    pts.give(it, t)
                prepare_sum()
                gemm("xo", 0, h_hi, h_lo, T, lambda k: o_rdy[k], add_to_x)

    def mlp():
        with ExitStack() as st:
            h_ready = norm_x(lambda k: param("norm_mlp_g", k, k + 1))
            fence()
            background[0] = modulation(st)
            background_pace[0] = 3
            f_hi = sb(st, "mlp_hi", [P, 8, T], F32R)
            f_lo = sb(st, "mlp_lo", [P, 8, T], F32R)
            relu = tmps
            hidden_free = [None]
            for blk in range(F1 // D):
                f_ready = {}

                def take_hidden(n, ps, tok):
                    i, r, rd = relu.take()
                    a = act.op(lambda e: e.activation(r[:, :], ps, ACT.Relu), [tok] + list(rd))
                    t = dve.op(lambda e: e.tensor_tensor(r[:, :], r[:, :], r[:, :], ALU.mult), [a])
                    f_ready[n] = split(f_hi[:, n, :], f_lo[:, n, :], r[:, :], [t, hidden_free[0]])
                    relu.give(i, f_ready[n])
                    return [a]

                gemm("mlp1", 0, h_hi, h_lo, T, lambda k: h_ready[k], take_hidden, panels=(blk * 4, blk * 4 + 4))
                if blk == F1 // D - 1:
                    prepare_sum()
                gemm("mlp2", blk, f_hi, f_lo, T, lambda k: f_ready[k], add_to_x)
                hidden_free[0] = pe.last()
            background_pace[0] = 0
            for _ in background[0]:
                pass
            finish_block_one()
            fence()

    def modulation(st):
        sil = sb(st, "sil", [P, 16])
        c_in = prm[:, PARAM_AT["c"][0]:PARAM_AT["c"][0] + 16]
        a = act.op(lambda e: e.activation(sil[:, :], c_in, ACT.Tanh, scale=0.5))
        t = dve.op(lambda e: e.scalar_tensor_tensor(out=sil[:, :], in0=sil[:, :], scalar=1.0, in1=c_in,
                                                    op0=ALU.add, op1=ALU.mult), [a])
        t_sil = dve.op(lambda e: e.tensor_scalar(sil[:, :], sil[:, :], 0.5, None, ALU.mult), [t])
        AW = 1024
        N_BUF = 3
        wbuf = [sb(st, f"ada_w{i}", [P, 2, AW]) for i in range(N_BUF)]
        ring_sems = [top.enter_context(nc.semaphore(f"ada_loaded{i}")) for i in range(N_BUF)]
        accs = Ring([sb(st, f"ada_acc{i}", [P, AW]) for i in range(2)])
        acc_c = sb(st, "ada_accc", [P, AW])
        w_free = [everything()] * N_BUF
        wanted = [(layer, j, kp) for layer in range(2) for j in range(6) for kp in range(DT // 2)]

        def fetch(n):
            if n < len(wanted):
                layer, j, kp = wanted[n]
                slot = n % N_BUF
                pool.wait(w_free[slot])
                src = dram[f"ada_w{layer}"][j, kp]
                pool.items.append(lambda e: e.dma_start(wbuf[slot][:, :, :], src).then_inc(ring_sems[slot], 16))

        for n in range(N_BUF - 1):
            fetch(n)
        t_prev = [None, None]
        for n, (layer, j, kp) in enumerate(wanted):
            fetch(n + N_BUF - 1)
            ctx_too = layer == 0 and j < 2
            slot = n % N_BUF
            landed = (ring_sems[slot], 16 * (n // N_BUF + 1))
            if kp == 0:
                i, acc, rd = accs.take()
                acc_c_free = pe.last()
            for kk in range(2):
                k = 2 * kp + kk
                for which, dst in ((0, acc), (1, acc_c)) if ctx_too else ((0, acc),):
                    w = wbuf[slot][:, kk, :]
                    col = sil[:, 8 * which + k:8 * which + k + 1]
                    if k == 0:
                        t_prev[which] = dve.op(lambda e, dst=dst, w=w, col=col: e.tensor_scalar(
                            dst[:, :], w, col, None, ALU.mult), [landed, t_sil, acc_c_free] + list(rd))
                    else:
                        t_prev[which] = dve.op(lambda e, dst=dst, w=w, col=col: e.scalar_tensor_tensor(
                            out=dst[:, :], in0=w, scalar=col, in1=dst[:, :], op0=ALU.mult, op1=ALU.add),
                            [landed, t_prev[which]])
                    if (which, kk) != (int(ctx_too), 1):
                        yield
            w_free[slot] = [t_prev[which] for which in range(2)]
            if kp < DT // 2 - 1:
                yield
                continue
            yield
            yield
            held = []
            for which, src_acc in ((0, acc), (1, acc_c)) if ctx_too else ((0, acc),):
                b, bank, free = work_banks.take()
                for c in range(8):
                    tok = mm(bank[:, c:c + 1], src_acc[:, c * P:(c + 1) * P], const("ones")[:, 0:1],
                             after=[t_prev[which]] + list(free), signal=(c == 7))
                held.append((b, bank, which, tok))
            accs.give(i, tok)
            yield
            yield
            for b, bank, which, tok in held:
                at = 96 + 8 * j if which else 48 * layer + 8 * j
                bias = param(f"ada_b{layer}", 8 * j, 8 * j + 8)
                td = dve.op(lambda e, bank=bank, at=at, bias=bias: e.tensor_tensor(
                    mod[:, at:at + 8], bank[:, 0:8], bias, ALU.add), [tok])
                work_banks.give(b, td)
            yield
        for at, gain in ((8, "norm1_g0"), (32, "norm2_g0"), (56, "norm1_g1"), (80, "norm2_g1"), (104, "norm1_g0")):
            td = dve.op(lambda e, at=at, gain=gain: e.scalar_tensor_tensor(
                out=mod[:, at:at + 8], in0=mod[:, at:at + 8], scalar=1.0, in1=param(gain),
                op0=ALU.add, op1=ALU.mult), [td])
        lm = prm[0:64, PARAM_AT["lam"][0]:PARAM_AT["lam"][0] + 4].rearrange("p (a b) -> p a b", b=2)
        pr = sb(st, "lam_pr", [64, 2])
        t = dve.op(lambda e: e.tensor_tensor(pr[:, :], lm[:, :, 0], lm[:, :, 1], ALU.mult))
        b, bank, free = work_banks.take()
        t = mm(bank[:, 0:2], const("ones")[0:64, :], pr[:, :], after=[t] + list(free))
        a = act.op(lambda e, bank=bank: e.activation(lam_col[:, 0:2], bank[:, 0:2], ACT.Exp), [t])
        work_banks.give(b, a)
        t = dve.op(lambda e: e.tensor_tensor(lam_col[:, 2:3], lam_col[:, 1:2], lam_col[:, 0:1], ALU.subtract), [a])
        dve.op(lambda e: e.tensor_scalar(lam_col[:, 3:4], lam_col[:, 2:3], -LAM_INIT, None, ALU.add), [t])

    def add_gated(layer, j):
        def take(n, ps, tok):
            g = mod[:, 48 * layer + 8 * j + n:48 * layer + 8 * j + n + 1]
            t = dve.op(lambda e: e.scalar_tensor_tensor(out=x_t[:, n, :], in0=ps, scalar=g, in1=x_t[:, n, :],
                                                        op0=ALU.mult, op1=ALU.add), [tok, x_tok.get(n)])
            x_written(n, t)
            return [t]
        return take

    def mod_col(at):
        return lambda k: mod[:, at + k:at + k + 1]

    def swiglu(layer):
        with ExitStack() as st:
            base = 48 * layer
            h_ready = norm_x(mod_col(base + 32), mod_col(base + 24))
            fence()
            f_hi = sb(st, f"ffn_hi{layer}", [P, 8, T], F32R)
            f_lo = sb(st, f"ffn_lo{layer}", [P, 8, T], F32R)
            tmp = tmps
            hidden_free = [None]
            for blk, (k0, nk) in enumerate(k_blocks(F2)):
                f_ready, held = {}, {}

                def take_hidden(n, ps, tok):
                    f, part = n // 2, n % 2
                    if part == 0:
                        i, y, rd = tmp.take()
                        a = act.op(lambda e: e.activation(y[:, :], ps, ACT.Tanh, scale=0.5), [tok] + list(rd))
                        t = dve.op(lambda e: e.scalar_tensor_tensor(out=y[:, :], in0=y[:, :], scalar=1.0, in1=ps,
                                                                    op0=ALU.add, op1=ALU.mult), [a])
                        held[f] = (i, y, t)
                        return [t]
                    i, y, t = held.pop(f)
                    t = dve.op(lambda e: e.scalar_tensor_tensor(out=y[:, :], in0=y[:, :], scalar=0.5, in1=ps,
                                                                op0=ALU.mult, op1=ALU.mult), [t, tok])
                    f_ready[f] = split(f_hi[:, f, :], f_lo[:, f, :], y[:, :], [t, hidden_free[0]])
                    tmp.give(i, f_ready[f])
                    return [t]

                gemm(f"ffn1_{layer}", 0, h_hi, h_lo, T, lambda k: h_ready[k], take_hidden, panels=(k0, k0 + nk))
                if k0 + nk == F2 // P:
                    prepare_sum()
                gemm(f"ffn2_{layer}", blk, f_hi, f_lo, T, lambda k: f_ready[k], add_gated(layer, 5))
                hidden_free[0] = pe.last()

    def diff_attention():
        NK = CTX + T
        KT = NK // P
        with ExitStack() as outer:
            k_all = sb(outer, "da_k", [P, DA_H, NK])
            v_all = sb(outer, "da_v", [P, KT, D])
            q = sb(outer, "da_q", [P, DA_H, T])
            with ExitStack() as st:
                c_hi = sb(st, "c_hi", [P, DT, CTX], F32R)
                c_lo = sb(st, "c_lo", [P, DT, CTX], F32R)
                with ExitStack() as s2:
                    ctx_t = sb(s2, "ctx_t", [P, DT, CTX])
                    fence()
                    tc = load(ctx_t[:, :, :], dram["ctx_t"].rearrange("(k p) t -> p k t", p=P),
                              after=everything())
                    act.wait([tc])
                    dve.wait([tc])
                    h_ready = norm_x(mod_col(8), mod_col(0))
                    c_ready = norm_other(lambda k: ctx_t[:, k, :], mod_col(104), mod_col(96), CTX, c_hi, c_lo)
                    fence()
                with ExitStack() as s2:
                    cosb = sb(s2, "rope_cos", [P, T])
                    sinb = sb(s2, "rope_sin", [P, T])
                    fence()
                    tr = [load(cosb[:, :], dram["rope_cos"], after=everything()),
                          load(sinb[:, :], dram["rope_sin"], after=everything())]
                    rr = Ring([sb(s2, f"rope_t{i}", [P, 2, T]) for i in range(1)])

                    def rope_into(dst):
                        def take(n, ps, tok):
                            i, buf, rd = rr.take()
                            a = act.op(lambda e: e.activation(buf[:, 0, :], ps, ACT.Copy), [tok] + list(rd))
                            swap = [(p + 16) % 32 for p in range(32)]
                            t = dve.op(lambda e: e.stream_shuffle(buf[:, 1, :], buf[:, 0, :], swap), [a])
                            t1 = pool.op(lambda e: e.tensor_tensor(buf[:, 0, :], buf[:, 0, :], cosb[:, :], ALU.mult),
                                         [t] + tr)
                            t2 = dve.op(lambda e: e.tensor_tensor(buf[:, 1, :], buf[:, 1, :], sinb[:, :], ALU.mult),
                                        [t] + tr)
                            t = dve.op(lambda e: e.tensor_tensor(dst(n), buf[:, 0, :], buf[:, 1, :], ALU.add), [t1, t2])
                            rr.give(i, t)
                            return [a]
                        return take

                    for i in range(len(where["da_k"][0])):
                        hi, lo, nk, width = panel("da_k", 0, i)
                        for c in range(width // P):
                            n = 2 * i + c
                            cut = slice(c * P, (c + 1) * P)
                            w = [(hi[:, k, cut], lo[:, k, cut]) for k in range(nk)]
                            b, bank, free = gemm_banks.take()
                            tok = products(bank[:, 0:CTX], [(w[k], (c_hi[:, k, :], c_lo[:, k, :])) for k in range(nk)],
                                           after=list(free) + [c_ready[k] for k in range(nk)])
                            gemm_banks.give(b, act.op(lambda e, n=n, bank=bank: e.activation(
                                k_all[:, n, 0:CTX], bank[:, 0:CTX], ACT.Copy), [tok]))
                            b, bank, free = gemm_banks.take()
                            tok = products(bank[:, :], [(w[k], (h_hi[:, k, :], h_lo[:, k, :])) for k in range(nk)],
                                           after=list(free) + [h_ready[k] for k in range(nk)])
                            if c == width // P - 1:
                                tok = end_panel()
                            gemm_banks.give(b, *rope_into(lambda n: k_all[:, n, CTX:NK])(n, bank[:, :], tok))
                    for i in range(len(where["da_v"][0])):
                        hi, lo, nk, width = panel("da_v", 0, i)
                        for m in range(KT):
                            a_hi, a_lo, at = (c_hi, c_lo, m) if m < CTX // P else (h_hi, h_lo, m - CTX // P)
                            cut = slice(at * P, (at + 1) * P)
                            b, bank, free = gemm_banks.take()
                            tok = products(bank[:, 0:width], [((a_hi[:, k, cut], a_lo[:, k, cut]),
                                                               (hi[:, k, :], lo[:, k, :])) for k in range(nk)],
                                           after=free)
                            if m == KT - 1:
                                tok = end_panel()
                            gemm_banks.give(b, act.op(lambda e, m=m, i=i, bank=bank: e.activation(
                                v_all[:, m, i * PW:(i + 1) * PW], bank[:, 0:PW], ACT.Copy), [tok]))
                    gemm("da_q", 0, h_hi, h_lo, T, lambda k: h_ready[k], rope_into(lambda n: q[:, n, :]))
                    fence()
            attend(outer, q, k_all, v_all, NK, KT)
            prepare_sum()
            gemm("da_o", 0, h_hi, h_lo, T, lambda k: None, add_gated(0, 2))

    def attend(s2, q, k_all, v_all, NK, KT):
        fence()
        scale = 64 ** -0.5
        pm = Ring([sb(s2, f"da_p{i}", [P, 2, NK]) for i in range(3)])
        pt = sb(s2, "da_pt", [P, KT, T])
        stat = Ring([sb(s2, f"da_stat{i}", [P, 12]) for i in range(3)])
        score_banks = Ring([banks[0:3], banks[3:6]])
        other_banks = Ring(banks[6:8])
        pt_free = [None]
        t_pt = [None]

        def scores(h, m):
            ip, p, rdp = pm.take()
            is_, s, rds = stat.take()
            b, (bk0, bk1, bk2), free = score_banks.take()
            tail = bk2[:, :].rearrange("p (a k) -> p a k", a=2)
            cut = slice(m * P, (m + 1) * P)
            side = lambda mp: (q[64 * mp:64 * mp + 64, h, cut], k_all[64 * mp:64 * mp + 64, h, :])
            (q0, k0), (q1, k1) = side(0), side(1)
            t = mm(tail[:, 0, :], q0, k0[:, 512:768], after=free)
            mm(bk1[:, :], q1, k1[:, 0:512], signal=False)
            mm(bk0[:, :], q0, k0[:, 0:512], signal=False)
            t_mm = mm(tail[:, 1, :], q1, k1[:, 512:768], after=[t])
            dve.wait(rds)
            for mp, bk in ((0, bk0), (1, bk1)):
                t1 = dve.op(lambda e, bk=bk, mp=mp: e.tensor_reduce(s[:, mp:mp + 1], bk[:, :], AX, ALU.max),
                            [t_mm])
            t2 = dve.op(lambda e: e.tensor_reduce(s[:, 2:4], tail, AX, ALU.max), [t_mm])
            t = dve.op(lambda e: e.tensor_tensor(s[:, 0:2], s[:, 0:2], s[:, 2:4], ALU.max), [t1, t2])
            t = dve.op(lambda e: e.tensor_scalar(s[:, 4:6], s[:, 0:2], -scale, None, ALU.mult), [t])
            for mp, bk in ((0, bk0), (1, bk1)):
                act.op(lambda e, bk=bk, mp=mp: e.activation(
                    p[:, mp, 0:512], bk[:, :], ACT.Exp, bias=s[:, 4 + mp:5 + mp], scale=scale,
                    accum_out=s[:, 6 + mp:7 + mp]), [t] + list(rdp))
                a = act.op(lambda e, mp=mp: e.activation(
                    p[:, mp, 512:768], tail[:, mp, :], ACT.Exp, bias=s[:, 4 + mp:5 + mp], scale=scale,
                    accum_out=s[:, 8 + mp:9 + mp]))
            score_banks.give(b, a)
            return ip, p, is_, s, a

        def combine(unit):
            ip, p, is_, s, a = unit
            t = dve.op(lambda e: e.tensor_tensor(s[:, 6:8], s[:, 6:8], s[:, 8:10], ALU.add), [a])
            t = dve.op(lambda e: e.reciprocal(s[:, 10:12], s[:, 6:8]), [t])
            t2 = dve.op(lambda e: e.tensor_scalar(p[:, 0, :], p[:, 0, :], s[:, 10:11], None, ALU.mult), [t])
            t = dve.op(lambda e: e.tensor_tensor(s[:, 11:12], s[:, 11:12], lam_col[:, 3:4], ALU.mult), [t])
            t_p = dve.op(lambda e: e.scalar_tensor_tensor(
                out=p[:, 0, :], in0=p[:, 1, :], scalar=s[:, 11:12], in1=p[:, 0, :], op0=ALU.mult, op1=ALU.add),
                [t, t2])
            stat.give(is_, t_p)
            return t_p

        def turn(m, unit, t_p):
            ip, p, is_, s, a = unit
            for half in range(2):
                b, bank, free = other_banks.take()
                for j in range(3):
                    kt = 3 * half + j
                    t = transpose(bank[:, j * P:(j + 1) * P], p[:, 0, kt * P:(kt + 1) * P],
                                  after=[t_p] + list(free), signal=(j == 2))
                t_pt[0] = act.op(lambda e, bank=bank, half=half: e.activation(
                    pt[:, 3 * half:3 * half + 3, m * P:(m + 1) * P],
                    bank[:, 0:3 * P].rearrange("p (a b) -> p a b", a=3), ACT.Copy), [t, pt_free[0]])
                other_banks.give(b, t_pt[0])
            pm.give(ip, t)

        def values(h):
            b, bank, free = other_banks.take()
            for kt in range(KT):
                t = mm(bank[:, :], v_all[:, kt, h * P:(h + 1) * P], pt[:, kt, :], start=(kt == 0),
                       stop=(kt == KT - 1), after=[t_pt[0]] + list(free), signal=(kt == KT - 1))
            pt_free[0] = t
            iy, y, rdy = tmps.take()
            iq, sq, rdq = tmps.take()
            ty = act.op(lambda e: e.activation(y[:, :], bank[:, :], ACT.Copy), [t] + list(rdy))
            ts = act.op(lambda e: e.activation(sq[:, :], y[:, :], ACT.Square), [ty] + list(rdq))
            other_banks.give(b, ty)
            return h, iy, y, iq, sq, ts

        def head_norm(state):
            h, iy, y, iq, sq, ts = state
            b, bank, free = other_banks.take()
            t = mm(bank[:, :], const("ones"), sq[:, :], after=[ts] + list(free))
            t = act.op(lambda e: e.activation(sq[:, :], bank[:, :], ACT.Sqrt, bias=param("eps"), scale=1.0 / P), [t])
            other_banks.give(b, t)
            t = dve.op(lambda e: e.reciprocal(sq[:, :], sq[:, :]), [t])
            t = dve.op(lambda e: e.scalar_tensor_tensor(out=y[:, :], in0=y[:, :], scalar=param("subln_g"),
                                                        in1=sq[:, :], op0=ALU.mult, op1=ALU.mult), [t])
            t = dve.op(lambda e: e.tensor_scalar(y[:, :], y[:, :], 1.0 - LAM_INIT, None, ALU.mult), [t])
            t = split(h_hi[:, h, :], h_lo[:, h, :], y[:, :], [t])
            tmps.give(iy, t)
            tmps.give(iq, t)

        units = [(h, m) for h in range(DA_H) for m in range(T // P)]
        issued, combined, waiting = [], [], None
        for n in range(len(units) + 2):
            if n >= 2:
                h, m = units[n - 2]
                turn(m, issued[n - 2], combined[n - 2])
            if 1 <= n <= len(units):
                combined.append(combine(issued[n - 1]))
            if n < len(units):
                issued.append(scores(*units[n]))
            if n >= 2 and m == 1 and waiting:
                head_norm(waiting)
                waiting = None
            if n >= 2 and m == T // P - 1:
                waiting = values(h)
        head_norm(waiting)
        fence()

    def short_conv():
        with ExitStack() as st:
            h_ready = norm_x(mod_col(56), mod_col(48))
            conv = sb(st, "sc_conv", [P, DT, T])
            f_hi = sb(st, "sc_hi", [P, 8, T], F32R)
            f_lo = sb(st, "sc_lo", [P, 8, T], F32R)
            zs = [sb(st, f"sc_z{i}", [P, T + 2]) for i in range(2)]
            fence()
            pads = []
            for z in zs:
                pool.op(lambda e, z=z: e.memset(z[:, 0:1], 0.0))
                pads.append(pool.op(lambda e, z=z: e.memset(z[:, T + 1:T + 2], 0.0)))
            ring = Ring(zs)
            ring.free = [(p,) for p in pads]
            held, made = {}, {}

            def take_cu(n, ps, tok):
                f, part = n // 2, n % 2
                if part == 0:
                    i, z, rd = ring.take()
                    a = act.op(lambda e: e.activation(z[:, 1:T + 1], ps, ACT.Copy), [tok] + list(rd))
                    held[f] = (i, z, a)
                    return [a]
                i, z, a = held.pop(f)
                t0 = dve.op(lambda e: e.tensor_tensor(z[:, 1:T + 1], z[:, 1:T + 1], ps, ALU.mult), [a, tok])
                w = lambda j: param("sc_conv_w", 3 * f + j, 3 * f + j + 1)
                t = dve.op(lambda e: e.tensor_scalar(conv[:, f, :], z[:, 0:T], w(0), None, ALU.mult), [t0])
                for j in range(1, 3):
                    t = dve.op(lambda e, j=j: e.scalar_tensor_tensor(
                        out=conv[:, f, :], in0=z[:, j:j + T], scalar=w(j), in1=conv[:, f, :],
                        op0=ALU.mult, op1=ALU.add), [t])
                ring.give(i, t)
                made[f] = t
                return [t0]

            gemm("sc_cu", 0, h_hi, h_lo, T, lambda k: h_ready[k], take_cu)
            f_ready = {}

            def take_b(n, ps, tok):
                t = dve.op(lambda e: e.tensor_tensor(conv[:, n, :], conv[:, n, :], ps, ALU.mult), [tok, made[n]])
                f_ready[n] = split(f_hi[:, n, :], f_lo[:, n, :], conv[:, n, :], [t])
                return [t]

            gemm("sc_b", 0, h_hi, h_lo, T, lambda k: h_ready[k], take_b)
            prepare_sum()
            gemm("sc_o", 0, f_hi, f_lo, T, lambda k: f_ready[k], add_gated(1, 2))

    def finish_block_one():
        r = rstd_of_x()
        for k in range(DT):
            x_tok[k] = dve.op(lambda e, k=k: e.scalar_tensor_tensor(
                out=x_t[:, k, :], in0=x_t[:, k, :], scalar=param("norm_final_g", k, k + 1), in1=rstd[:, :],
                op0=ALU.mult, op1=ALU.mult), [r, x_tok[k]])
        rstd_free[0] = (x_tok[DT - 1],)
        prepare_sum()
        for k in range(DT):
            x_written(k, x_tok[k])

    def final():
        with ExitStack() as st:
            r = rstd_of_x()
            out_v = out_t.rearrange("(k p) t -> p k t", p=P)
            stored = top.enter_context(nc.semaphore("stored"))
            for k in range(DT):
                t = dve.op(lambda e, k=k: e.scalar_tensor_tensor(
                    out=x_t[:, k, :], in0=x_t[:, k, :], scalar=param("final_g", k, k + 1), in1=rstd[:, :],
                    op0=ALU.mult, op1=ALU.mult), [r])
                sp.wait([t])
                sp.items.append(lambda e, k=k: e.dma_start(out_v[:, k, :], x_t[:, k, :]).then_inc(stored, 16))
            sp.items.append(lambda e: e.wait_ge(stored, 16 * DT))

    mixer()
    cross_attention()
    mlp()
    diff_attention()
    swiglu(0)
    short_conv()
    swiglu(1)
    final()
    for q in engines + (sp,):
        q.flush()
    top.close()


def lay_params(inputs):
    f = lambda name: np.asarray(inputs[name])
    cols = lambda a: a.reshape(-1, P).T
    spread = lambda a: np.broadcast_to(a.reshape(1, -1), (P, a.size))
    lam = np.zeros((P, 4), np.float32)
    lam[0:64, :] = f("da_lambda_2")[0].T
    conv = f("gdn_conv_w")[0].reshape(4, 24, P).transpose(2, 1, 0).reshape(P, 96)
    sc = f("sc_conv_w_2")[0].reshape(3, 8, P).transpose(2, 1, 0).reshape(P, 24)
    table = {
        "norm_mix_g": cols(f("norm_mix_g")), "gdn_conv_w": conv, "a_log": spread(f("gdn_a_log")),
        "dt_bias": spread(f("gdn_dt_bias")), "gdn_norm_g": cols(f("gdn_norm_g")),
        "gla_b_gate": cols(f("gla_b_gate")), "gla_norm_g": cols(f("gla_norm_g")),
        "norm_xattn_g": cols(f("norm_xattn_g")), "norm_mem_g": cols(f("norm_mem_g")),
        "norm_mlp_g": cols(f("norm_mlp_g")), "norm_final_g": cols(f("norm_final_g")),
        "c": cols(f("c_2")), "c_ctx": cols(f("c_ctx_2")),
        "ada_b0": cols(f("ada_b_2")[0]), "ada_b1": cols(f("ada_b_2")[1]),
        "norm1_g0": cols(f("norm1_g_2")[0]), "norm1_g1": cols(f("norm1_g_2")[1]),
        "norm2_g0": cols(f("norm2_g_2")[0]), "norm2_g1": cols(f("norm2_g_2")[1]),
        "final_g": cols(f("final_g_2")), "lam": lam, "subln_g": cols(f("da_subln_g_2")), "sc_conv_w": sc,
        "eps": np.full((P, 1), EPS, np.float32), "eps4": np.full((P, 1), 4 * EPS, np.float32),
    }
    return np.concatenate([table[name] for name, _ in PARAM_WIDTHS], axis=1)


def shape_constants():
    i = np.arange(P)[:, None]
    j = np.arange(P)[None, :]

    def level(s, row, col):
        return (row // (2 * s) == col // (2 * s)) & (row % (2 * s) >= s) & (col % (2 * s) < s)

    made = {"ident": i == j, "ones": np.ones((P, P)), "incl_t": i <= j, "strict": i > j, "strict_t": i < j,
            "lvl1": level(1, i, j), "lvl1_t": level(1, j, i)}
    for s in (2, 4, 8, 16, 32, 64):
        made[f"lvl{s}_t"] = level(s, j, i)
    return np.concatenate([made[n].astype(np.float32) for n in CONSTS], axis=1)


def rope_constants():
    n = np.arange(T)
    inv = 1.0 / (10000.0 ** (np.arange(0, 32, 2, dtype=np.float32) / np.float32(32)))
    inv = inv.astype(np.float32)
    row, col = (n // 64).astype(np.float32), (n % 64).astype(np.float32)
    ang = np.concatenate([row[None, :] * inv[:, None], col[None, :] * inv[:, None]], 0).astype(np.float32)
    d = np.arange(P) % 64
    which = (d // 32) * 16 + d % 16
    sign = np.where(d % 32 < 16, -1.0, 1.0).astype(np.float32)
    return np.cos(ang)[which].astype(np.float32), (np.sin(ang)[which] * sign[:, None]).astype(np.float32)


def pack(weight, blocks, columns):
    parts = []
    for k0, nk in blocks:
        for cols in columns:
            w = weight[k0 * P:(k0 + nk) * P, cols]
            parts.append(w.reshape(nk, P, len(cols)).transpose(1, 0, 2).reshape(-1))
    return np.concatenate(parts)


def kernel(**inputs):
    import concourse.bacc as bacc
    from concourse.bass_utils import run_bass_kernel_spmd

    f = lambda name: np.asarray(inputs[name])
    cos, sin = rope_constants()
    arrays = {
        "x_t": np.ascontiguousarray(f("x")[0].T), "mem_t": np.ascontiguousarray(f("mem")[0].T),
        "ctx_t": np.ascontiguousarray(f("ctx_2")[0].T), "params": lay_params(inputs),
        "consts": shape_constants(), "rope_cos": cos, "rope_sin": sin,
        "gla_w2": np.ascontiguousarray(f("gla_w_gate2")[0]),
    }
    for layer in range(2):
        a = f("ada_w_2")[layer].reshape(4, 2, P, 6, D).transpose(3, 0, 2, 1, 4)
        arrays[f"ada_w{layer}"] = np.ascontiguousarray(a)
    for key, weight, blocks, columns in panel_plan():
        name, _, layer = weight.partition(".")
        arrays["pack_" + key] = pack(f(name)[int(layer or 0)], blocks, columns)

    nc = bacc.Bacc("TRN2", target_bir_lowering=False, num_devices=1)
    dram = {n: nc.dram_tensor("in_" + n, a.shape, F32, kind="ExternalInput").ap() for n, a in arrays.items()}
    out = nc.dram_tensor("out_t", (D, T), F32, kind="ExternalOutput").ap()
    build_program(nc, dram, out)
    result = run_bass_kernel_spmd(nc, [{"in_" + n: a for n, a in arrays.items()}], core_ids=[0])
    return np.ascontiguousarray(result.results[0]["out_t"].T)[None]
```
